# Optimizing a Trainium2 kernel written in Bass

```python
import jax
import jax.numpy as jnp
from jax import lax
import numpy as np

D_MODEL = 1024
BATCH = 1
SEQ = 1024
DEPTH = 2
DEC_BATCH = 1
DEC_SEQ = 64
PAST_LEN = 512

CHUNK = 64
HEAD_DIM = 64
N_EVEN = (DEPTH + 1) // 2
N_ODD = DEPTH // 2
EPS = 1e-6
ROPE_THETA = 10000.0

A_HEADS = 8
A_KV_HEADS = 2
IDX_HEADS = 8
IDX_DIM = 64
IDX_W_SCALE = (IDX_HEADS * IDX_DIM) ** -0.5
TOPK_MAX = 256
QBLOCK = 128

B_HEADS = 8
B_LEFT_CHUNKS = 8
B_WINDOW = B_LEFT_CHUNKS * CHUNK
B_MAX_REL = 128

C_HEADS = 16
C_KV_HEADS = 2
C_WINDOW = 128
C_LEFT_CHUNKS = C_WINDOW // CHUNK

D_FF = -(-8 * D_MODEL // (3 * 256)) * 256

EVEN_SIZES = (A_HEADS * HEAD_DIM, A_KV_HEADS * HEAD_DIM, A_KV_HEADS * HEAD_DIM,
              IDX_HEADS * IDX_DIM, IDX_DIM, IDX_HEADS,
              B_HEADS * HEAD_DIM, B_HEADS * HEAD_DIM, B_HEADS * HEAD_DIM)
EVEN_IN = (A_HEADS + 2 * A_KV_HEADS + 3 * B_HEADS) * HEAD_DIM + (IDX_HEADS + 1) * IDX_DIM + IDX_HEADS
EVEN_OUT = (A_HEADS + B_HEADS) * HEAD_DIM
ODD_SIZES = (C_HEADS * HEAD_DIM, C_KV_HEADS * HEAD_DIM, C_KV_HEADS * HEAD_DIM)
ODD_IN = (C_HEADS + 2 * C_KV_HEADS) * HEAD_DIM
ODD_OUT = C_HEADS * HEAD_DIM

kernel_name = 'hybrid_dsa_chunkband_swa_stream_step'

def rmsnorm(x, g):
    x32 = x.astype(jnp.float32)
    y = x32 * lax.rsqrt(jnp.mean(x32 * x32, axis=-1, keepdims=True) + EPS)
    return (y * g.astype(jnp.float32)).astype(x.dtype)

def rope(x, pos):
    half = x.shape[-1] // 2
    inv_freq = ROPE_THETA ** (-jnp.arange(half, dtype=jnp.float32) / half)
    ang = pos.astype(jnp.float32)[:, None] * inv_freq[None, :]
    cos = jnp.cos(ang)[:, None, :]
    sin = jnp.sin(ang)[:, None, :]
    x32 = x.astype(jnp.float32)
    x1, x2 = x32[..., :half], x32[..., half:]
    return jnp.concatenate([x1 * cos - x2 * sin, x2 * cos + x1 * sin], axis=-1).astype(x.dtype)

def split_cols(h, sizes):
    points = []
    acc = 0
    for s in sizes[:-1]:
        acc += s
        points.append(acc)
    return jnp.split(h, points, axis=-1)

def heads(t, n, d):
    return t.reshape(t.shape[0], t.shape[1], n, d)

def even_project(xn, pos, w_in, a_qn, a_kn, i_kn, b_qn, b_kn):
    aq, ak, av, iq, ik, iw, bq, bk, bv = split_cols(xn @ w_in, EVEN_SIZES)
    aq = rope(rmsnorm(heads(aq, A_HEADS, HEAD_DIM), a_qn), pos)
    ak = rope(rmsnorm(heads(ak, A_KV_HEADS, HEAD_DIM), a_kn), pos)
    av = heads(av, A_KV_HEADS, HEAD_DIM)
    iq = rope(heads(iq, IDX_HEADS, IDX_DIM), pos)
    ik = rope(rmsnorm(ik, i_kn)[:, :, None, :], pos)[:, :, 0, :]
    iw = iw * IDX_W_SCALE
    bq = rmsnorm(heads(bq, B_HEADS, HEAD_DIM), b_qn)
    bk = rmsnorm(heads(bk, B_HEADS, HEAD_DIM), b_kn)
    bv = heads(bv, B_HEADS, HEAD_DIM)
    return aq, ak, av, iq, ik, iw, bq, bk, bv

def odd_project(xn, pos, w_in, c_qn, c_kn):
    q, k, v = split_cols(xn @ w_in, ODD_SIZES)
    q = rope(rmsnorm(heads(q, C_HEADS, HEAD_DIM), c_qn), pos)
    k = rope(rmsnorm(heads(k, C_KV_HEADS, HEAD_DIM), c_kn), pos)
    v = heads(v, C_KV_HEADS, HEAD_DIM)
    return q, k, v

def dsa_attention(q, iq, iw, k, v, ik, q_pos, k_pos, topk):
    rel = jax.nn.relu(jnp.einsum('btnd,bsd->btns', iq.astype(jnp.float32), ik.astype(jnp.float32)))
    score = jnp.einsum('btns,btn->bts', rel, iw.astype(jnp.float32))
    admissible = (k_pos[None, :] // CHUNK) <= (q_pos[:, None] // CHUNK)
    score = jnp.where(admissible[None], score, -jnp.inf)
    sel_score, sel = lax.top_k(score, topk)
    valid = jnp.isfinite(sel_score)
    kg = jax.vmap(lambda kb, ib: kb[ib])(k, sel)
    vg = jax.vmap(lambda vb, ib: vb[ib])(v, sel)
    bn, t = q.shape[0], q.shape[1]
    qg = q.reshape(bn, t, A_KV_HEADS, A_HEADS // A_KV_HEADS, HEAD_DIM)
    logits = jnp.einsum('btkgd,btskd->btkgs', qg, kg).astype(jnp.float32) * HEAD_DIM ** -0.5
    logits = jnp.where(valid[:, :, None, None, :], logits, -jnp.inf)
    p = jax.nn.softmax(logits, axis=-1)
    out = jnp.einsum('btkgs,btskd->btkgd', p.astype(v.dtype), vg)
    return out.reshape(bn, t, A_HEADS * HEAD_DIM)

def band_attention(q, k, v, q_pos, k_pos, n_left, rel_bias, sinks):
    bn, c, t, h = q.shape[0], q.shape[1], q.shape[2], q.shape[3]
    kv = k.shape[3]
    g = h // kv
    l = k.shape[2]
    qc = q_pos // CHUNK
    kc = k_pos // CHUNK
    valid = ((k_pos[:, None, :] >= 0) & (kc[:, None, :] <= qc[:, :, None])
             & (kc[:, None, :] >= qc[:, :, None] - n_left))
    qg = q.reshape(bn, c, t, kv, g, HEAD_DIM)
    logits = jnp.einsum('bctkgd,bcskd->bckgts', qg, k).astype(jnp.float32) * HEAD_DIM ** -0.5
    if rel_bias is not None:
        ridx = jnp.clip(k_pos[:, None, :] - q_pos[:, :, None], -B_MAX_REL, B_MAX_REL) + B_MAX_REL
        bias = rel_bias.astype(jnp.float32)[:, ridx]
        bias = jnp.moveaxis(bias.reshape(kv, g, c, t, l), 2, 0)
        logits = logits + bias[None]
    logits = jnp.where(valid[None, :, None, None], logits, -jnp.inf)
    if sinks is None:
        p = jax.nn.softmax(logits, axis=-1)
    else:
        s = sinks.astype(jnp.float32).reshape(1, 1, kv, g, 1, 1)
        m = jnp.maximum(jnp.max(logits, axis=-1, keepdims=True), s)
        e = jnp.exp(logits - m)
        p = e / (jnp.sum(e, axis=-1, keepdims=True) + jnp.exp(s - m))
    out = jnp.einsum('bckgts,bcskd->bctkgd', p.astype(v.dtype), v)
    return out.reshape(bn, c, t, h * HEAD_DIM)

def to_band(x, n_left):
    bn, s = x.shape[0], x.shape[1]
    nc = s // CHUNK
    pad = [(0, 0), (n_left * CHUNK, 0)] + [(0, 0)] * (x.ndim - 2)
    xp = jnp.pad(x, pad).reshape(bn, nc + n_left, CHUNK, *x.shape[2:])
    band = jnp.stack([xp[:, j:j + nc] for j in range(n_left + 1)], axis=2)
    return band.reshape(bn, nc, (n_left + 1) * CHUNK, *x.shape[2:])

def band_prompt(q, k, v, n_left, rel_bias, sinks):
    bn, s = q.shape[0], q.shape[1]
    nc = s // CHUNK
    q_pos = jnp.arange(s, dtype=jnp.int32).reshape(nc, CHUNK)
    k_pos = ((jnp.arange(nc, dtype=jnp.int32)[:, None] - n_left) * CHUNK
             + jnp.arange((n_left + 1) * CHUNK, dtype=jnp.int32)[None, :])
    out = band_attention(q.reshape(bn, nc, CHUNK, *q.shape[2:]), to_band(k, n_left), to_band(v, n_left),
                         q_pos, k_pos, n_left, rel_bias, sinks)
    return out.reshape(bn, s, -1)

def band_sample(q, k_new, v_new, k_cache, v_cache, n_left, rel_bias, sinks):
    t = q.shape[1]
    w = k_cache.shape[1]
    q_pos = PAST_LEN + jnp.arange(t, dtype=jnp.int32)
    k_pos = jnp.concatenate([PAST_LEN - w + jnp.arange(w, dtype=jnp.int32), q_pos])
    k = jnp.concatenate([k_cache, k_new], axis=1)[:, None]
    v = jnp.concatenate([v_cache, v_new], axis=1)[:, None]
    out = band_attention(q[:, None], k, v, q_pos[None], k_pos[None], n_left, rel_bias, sinks)
    return out[:, 0]

def to_qblocks(t, nb):
    return jnp.moveaxis(t.reshape(t.shape[0], nb, QBLOCK, *t.shape[2:]), 1, 0)

def swiglu(x, w_in, w_out):
    gate, up = jnp.split(x @ w_in, 2, axis=-1)
    return (jax.nn.silu(gate) * up) @ w_out

def setup_inputs(seed: int = 0) -> dict:
    key = jax.random.key(seed)
    ks = jax.random.split(key, 32)

    def nrm(k, shape, scale=1.0):
        return jax.random.normal(k, shape, jnp.float32) * scale

    def gain(k, shape):
        return 1.0 + 0.02 * jax.random.normal(k, shape, jnp.float32)

    wb = min(B_WINDOW, PAST_LEN)
    wc = min(C_WINDOW, PAST_LEN)
    return {
        'x_prompt': nrm(ks[0], (BATCH, SEQ, D_MODEL)),
        'x_sample': nrm(ks[1], (DEC_BATCH, DEC_SEQ, D_MODEL)),
        'cache_a_k': nrm(ks[2], (N_EVEN, DEC_BATCH, PAST_LEN, A_KV_HEADS, HEAD_DIM)),
        'cache_a_v': nrm(ks[3], (N_EVEN, DEC_BATCH, PAST_LEN, A_KV_HEADS, HEAD_DIM)),
        'cache_a_kidx': nrm(ks[4], (N_EVEN, DEC_BATCH, PAST_LEN, IDX_DIM)),
        'cache_b_k': nrm(ks[5], (N_EVEN, DEC_BATCH, wb, B_HEADS, HEAD_DIM)),
        'cache_b_v': nrm(ks[6], (N_EVEN, DEC_BATCH, wb, B_HEADS, HEAD_DIM)),
        'cache_c_k': nrm(ks[7], (N_ODD, DEC_BATCH, wc, C_KV_HEADS, HEAD_DIM)),
        'cache_c_v': nrm(ks[8], (N_ODD, DEC_BATCH, wc, C_KV_HEADS, HEAD_DIM)),
        'norm_mix': gain(ks[9], (DEPTH, D_MODEL)),
        'norm_ffn': gain(ks[10], (DEPTH, D_MODEL)),
        'w_in_even': nrm(ks[11], (N_EVEN, D_MODEL, EVEN_IN), D_MODEL ** -0.5),
        'w_out_even': nrm(ks[12], (N_EVEN, EVEN_OUT, D_MODEL), EVEN_OUT ** -0.5),
        'a_q_norm': gain(ks[13], (N_EVEN, HEAD_DIM)),
        'a_k_norm': gain(ks[14], (N_EVEN, HEAD_DIM)),
        'idx_k_norm': gain(ks[15], (N_EVEN, IDX_DIM)),
        'b_q_norm': gain(ks[16], (N_EVEN, HEAD_DIM)),
        'b_k_norm': gain(ks[17], (N_EVEN, HEAD_DIM)),
        'b_rel_bias': nrm(ks[18], (N_EVEN, B_HEADS, 2 * B_MAX_REL + 1), 0.1),
        'w_in_odd': nrm(ks[19], (N_ODD, D_MODEL, ODD_IN), D_MODEL ** -0.5),
        'w_out_odd': nrm(ks[20], (N_ODD, ODD_OUT, D_MODEL), ODD_OUT ** -0.5),
        'c_q_norm': gain(ks[21], (N_ODD, HEAD_DIM)),
        'c_k_norm': gain(ks[22], (N_ODD, HEAD_DIM)),
        'c_sinks': nrm(ks[23], (N_ODD, C_HEADS), 0.5),
        'w_ffn_in': nrm(ks[24], (DEPTH, D_MODEL, 2 * D_FF), D_MODEL ** -0.5),
        'w_ffn_out': nrm(ks[25], (DEPTH, D_FF, D_MODEL), D_FF ** -0.5),
    }

def reference(x_prompt, x_sample, cache_a_k, cache_a_v, cache_a_kidx, cache_b_k, cache_b_v,
              cache_c_k, cache_c_v, norm_mix, norm_ffn, w_in_even, w_out_even, a_q_norm, a_k_norm,
              idx_k_norm, b_q_norm, b_k_norm, b_rel_bias, w_in_odd, w_out_odd, c_q_norm, c_k_norm,
              c_sinks, w_ffn_in, w_ffn_out):
    seq = x_prompt.shape[1]
    t_new = x_sample.shape[1]
    pos_p = jnp.arange(seq, dtype=jnp.int32)
    pos_s = PAST_LEN + jnp.arange(t_new, dtype=jnp.int32)
    k_pos_s = jnp.arange(PAST_LEN + t_new, dtype=jnp.int32)
    topk_p = min(TOPK_MAX, seq // 4)
    topk_s = min(TOPK_MAX, (PAST_LEN + t_new) // 4)
    nb = seq // QBLOCK
    keep_b = min(B_WINDOW, seq)
    keep_c = min(C_WINDOW, seq)
    pa_k, pa_v, pa_i, pb_k, pb_v, pc_k, pc_v = [], [], [], [], [], [], []
    sa_k, sa_v, sa_i, sb_k, sb_v, sc_k, sc_v = [], [], [], [], [], [], []

    hp, hs = x_prompt, x_sample
    for layer in range(DEPTH):
        li = layer // 2
        xp = rmsnorm(hp, norm_mix[layer])
        xs = rmsnorm(hs, norm_mix[layer])
        if layer % 2 == 0:
            ew = (w_in_even[li], a_q_norm[li], a_k_norm[li], idx_k_norm[li], b_q_norm[li], b_k_norm[li])
            aq, ak, av, iq, ik, iw, bq, bk, bv = even_project(xp, pos_p, *ew)

            def attend_block(blk, ak=ak, av=av, ik=ik):
                qb, iqb, iwb, pb = blk
                return dsa_attention(qb, iqb, iwb, ak, av, ik, pb, pos_p, topk_p)

            out_a = lax.map(attend_block, (to_qblocks(aq, nb), to_qblocks(iq, nb), to_qblocks(iw, nb),
                                           pos_p.reshape(nb, QBLOCK)))
            out_a = jnp.moveaxis(out_a, 0, 1).reshape(hp.shape[0], seq, A_HEADS * HEAD_DIM)
            out_b = band_prompt(bq, bk, bv, B_LEFT_CHUNKS, b_rel_bias[li], None)
            mix_p = jnp.concatenate([out_a, out_b], axis=-1) @ w_out_even[li]
            pa_k.append(ak)
            pa_v.append(av)
            pa_i.append(ik)
            pb_k.append(bk[:, seq - keep_b:])
            pb_v.append(bv[:, seq - keep_b:])
            aq, ak, av, iq, ik, iw, bq, bk, bv = even_project(xs, pos_s, *ew)
            k_all = jnp.concatenate([cache_a_k[li], ak], axis=1)
            v_all = jnp.concatenate([cache_a_v[li], av], axis=1)
            i_all = jnp.concatenate([cache_a_kidx[li], ik], axis=1)
            out_a = dsa_attention(aq, iq, iw, k_all, v_all, i_all, pos_s, k_pos_s, topk_s)
            out_b = band_sample(bq, bk, bv, cache_b_k[li], cache_b_v[li], B_LEFT_CHUNKS, b_rel_bias[li], None)
            mix_s = jnp.concatenate([out_a, out_b], axis=-1) @ w_out_even[li]
            sa_k.append(ak)
            sa_v.append(av)
            sa_i.append(ik)
            sb_k.append(bk)
            sb_v.append(bv)
        else:
            q, k, v = odd_project(xp, pos_p, w_in_odd[li], c_q_norm[li], c_k_norm[li])
            mix_p = band_prompt(q, k, v, C_LEFT_CHUNKS, None, c_sinks[li]) @ w_out_odd[li]
            pc_k.append(k[:, seq - keep_c:])
            pc_v.append(v[:, seq - keep_c:])
            q, k, v = odd_project(xs, pos_s, w_in_odd[li], c_q_norm[li], c_k_norm[li])
            mix_s = band_sample(q, k, v, cache_c_k[li], cache_c_v[li], C_LEFT_CHUNKS, None, c_sinks[li]) @ w_out_odd[li]
            sc_k.append(k)
            sc_v.append(v)
        hp = hp + mix_p
        hs = hs + mix_s
        hp = hp + swiglu(rmsnorm(hp, norm_ffn[layer]), w_ffn_in[layer], w_ffn_out[layer])
        hs = hs + swiglu(rmsnorm(hs, norm_ffn[layer]), w_ffn_in[layer], w_ffn_out[layer])

    return (hp, hs,
            jnp.stack(pa_k), jnp.stack(pa_v), jnp.stack(pa_i), jnp.stack(pb_k), jnp.stack(pb_v),
            jnp.stack(pc_k), jnp.stack(pc_v),
            jnp.stack(sa_k), jnp.stack(sa_v), jnp.stack(sa_i), jnp.stack(sb_k), jnp.stack(sb_v),
            jnp.stack(sc_k), jnp.stack(sc_v))


_drawn_inputs = setup_inputs


def setup_inputs(seed=0):
    import zlib

    import numpy as np

    out = dict(_drawn_inputs(seed))
    spreads = {}
    factors = {'norm_ffn': 2.741,
     'a_q_norm': 8.0,
     'a_k_norm': 2.924,
     'idx_k_norm': 3.01,
     'b_q_norm': 8.0,
     'b_k_norm': 2.853,
     'b_rel_bias': 8.0,
     'c_q_norm': 29.027,
     'c_k_norm': 11.472,
     'c_sinks': 8.0,
     'cache_b_v': 53.839,
     'cache_c_k': 8.0,
     'cache_c_v': 8.0}
    for name, (base, spread) in spreads.items():
        noise = np.random.default_rng([zlib.crc32(name.encode()), seed]).standard_normal(out[name].shape)
        drawn = base * np.exp(spread * noise) if base else spread * noise
        out[name] = jnp.asarray(drawn.astype(out[name].dtype))
    for name, factor in factors.items():
        out[name] = (out[name] * factor).astype(out[name].dtype)
    return out
```

```python
from contextlib import ExitStack

import concourse.bass as bass
import numpy as np
from concourse import mybir

F32 = mybir.dt.float32
F32R = mybir.dt.float32r
ALU = mybir.AluOpType
ACT = mybir.ActivationFunctionType
AX = mybir.AxisListType

P = 128
D = 1024
KT = D // P
CHUNK = 64
HD = 64
SAMPLE, PROMPT, PAST = 64, 1024, 512
NTOK = SAMPLE + PROMPT
TILES = 1 + PROMPT // P
CUTS = [(0, 384), (384, 352), (736, 352)]
EPS = 1e-6
D_FF = 2816
FGROUPS = D_FF // 256
TOPK_P, TOPK_S = 256, 144
MASKED = -1e30
TAKEN = -3e38
SW = 512
IDX_SCALE = 512 ** -0.5

EVEN_GROUPS = [("ikv", 328, 3, 3), ("iq", 512, 0, 8), ("aq", 512, 8, 8),
               ("bq", 512, 8, 0), ("bk", 512, 8, 0), ("bv", 512, 0, 0)]
ODD_GROUPS = [("cq0", 512, 8, 8), ("cq1", 512, 8, 8), ("ckv", 256, 2, 2)]


def tile_cols(t):
    return (0, P) if t == 0 else (SAMPLE + P * (t - 1), SAMPLE + P * t)


def cuts_for(col_end):
    return 1 + max(i for i, (c0, _) in enumerate(CUTS) if c0 < col_end)


TOPK_TILES = [0] + list(range(3, TILES))


def score_width(t):
    return PAST + SAMPLE if t == 0 else P * t


PIECES = []
for _t in TOPK_TILES:
    _n = score_width(_t)
    _parts = [(0, _n)] if _n <= 512 else [(0, _n // 2), (_n // 2, _n // 2)]
    for _h in range(8):
        for _i, (_c, _w) in enumerate(_parts):
            PIECES.append((_t, _h, _c, _w, _h == 7 and _i == len(_parts) - 1))
PIECE_END = {p[0]: i + 1 for i, p in enumerate(PIECES)}
SCORE_OFF = {}
_o = 0
for _t in TOPK_TILES:
    SCORE_OFF[_t] = _o
    _o += score_width(_t)
SCORE_COLS = _o
ROUNDS = []
for _t in TOPK_TILES:
    _r = (TOPK_S if _t == 0 else TOPK_P) // 8
    ROUNDS += [(_t, i == _r - 1) for i in range(_r)]
ROUND_END = {r[0]: i + 1 for i, r in enumerate(ROUNDS)}
FIRST_PIECE_UNIT = 12


def pieces_by(u):
    return min(len(PIECES), max(0, (u - FIRST_PIECE_UNIT + 1) * 12 // 5))


class Job:
    def __init__(self, kind, t):
        self.kind, self.t = kind, t
        self.heads = 16 if kind == "C" else 8
        self.group = 4 if kind == "C" else 1
        self.steps = self.heads // self.group
        if kind == "A":
            self.blocks = list(range(8, 13)) if t == 0 else list(range(t))
        elif kind == "B":
            self.blocks = list(range(8, 13)) if t == 0 else list(range(max(0, t - 5), t))
        else:
            self.blocks = [8, 9] if t == 0 else list(range(max(0, t - 2), t))
        self.width = P * len(self.blocks) - (P - SAMPLE if t == 0 else 0)


EVEN_JOBS = [Job(k, t) for k, t in [("A", 1), ("A", 2), ("B", 0), ("B", 1), ("A", 0), ("B", 2), ("A", 3),
             ("B", 3), ("A", 4), ("B", 4), ("B", 5), ("A", 5), ("B", 6), ("A", 6), ("B", 7), ("B", 8),
             ("A", 7), ("A", 8)]]
ODD_JOBS = [Job("C", t) for t in range(TILES)]


class Plan:

    def __init__(self, jobs):
        self.jobs = jobs
        self.steps = [(j, i) for j, job in enumerate(jobs) for i in range(job.steps)]
        self.first = [sum(x.steps for x in jobs[:j]) for j in range(len(jobs) + 1)]
        self.pt_groups = []
        for j, i in self.steps:
            job = jobs[j]
            units = [(g, b) for g in range(job.group) for b in range(len(job.blocks))]
            self.pt_groups.append([units[k:k + 4] for k in range(0, len(units), 4)])
        self.pt_base = [sum(len(g) for g in self.pt_groups[:s]) for s in range(len(self.steps) + 1)]
        self.uses = []
        for s in range(-1, len(self.steps) + 4):
            self.uses += self.at_slot(s)
        self.use_no = {u: n for n, u in enumerate(self.uses)}

    def bank_uses(self, j, what):
        job = self.jobs[j]
        if what == "k":
            return [("k", j, 0)]
        return [(what, j, i) for i in range(2 if job.kind == "C" else 1)]

    def at_slot(self, s):
        if s == -1:
            return self.bank_uses(0, "q") + self.bank_uses(0, "k")
        out = []
        for j, job in enumerate(self.jobs):
            if j + 1 < len(self.jobs) and s == self.first[j] + job.steps // 2:
                out += self.bank_uses(j + 1, "q")
            if j + 1 < len(self.jobs) and s == self.first[j] + job.steps // 2 + 1:
                out += self.bank_uses(j + 1, "k")
            if s == self.first[j + 1] + 3:
                out += self.bank_uses(j, "o")
        return out

    def count(self, kinds, use):
        return sum(1 for u in self.uses[:self.use_no[use] + 1] if u[0] in kinds)


EVEN_PLAN, ODD_PLAN = Plan(EVEN_JOBS), Plan(ODD_JOBS)


def rounds_by_unit(u):
    n = 0
    for v in range(u + 1):
        for _ in range(2):
            if n < len(ROUNDS) and pieces_by(v - 3) >= PIECE_END[ROUNDS[n][0]]:
                n += 1
    return n


def rounds_by_step(s, done):
    at, have = -1, done
    for j, job in enumerate(EVEN_JOBS):
        if job.kind != "A" or job.t in (1, 2):
            continue
        end, need = EVEN_PLAN.first[j] - 1, ROUND_END[job.t]
        if need <= have:
            continue
        if s < end:
            return have + (need - have) * (s - at) // (end - at)
        at, have = end, need
    return have


def band_block(b):
    return (b - 8 if b >= 8 else 5 + b) % 6


def build(nc, a):
    ctx = ExitStack()
    with ctx:
        base = (nc.sbuf_base + 63) // 64 * 64
        top = nc.sbuf_usable_end
        RING = 16

        class Region:

            def __init__(self, *spans):
                self.spans = [list(s) for s in spans]

            def cut(self, name, shape, dt=F32):
                size = (int(np.prod(shape[1:])) * 4 + 31) // 32 * 32
                for s in self.spans:
                    if s[1] - s[0] >= size:
                        t = nc.alloc_sbuf_tensor_at(name, shape, dt, offset=s[0])
                        s[0] += size
                        return t
                raise ValueError(f"no room for {name}: {size} in {self.spans}")

        whole = Region((base, top))
        cos = whole.cut("cos", [P, TILES, HD])
        sin = whole.cut("sin", [P, TILES, HD])
        band_mask = whole.cut("band_mask", [P, 640])
        c_mask = whole.cut("c_mask", [P, 256])
        ident = whole.cut("ident", [P, P])
        ones = whole.cut("ones", [P, P])
        gains = {n: whole.cut(f"gain_{n}", [P, w]) for n, w in
                 (("ikv", 192), ("aq", 64), ("bq", 64), ("bk", 64), ("cq", 64), ("ck", 64))}
        gains_sw = {n: whole.cut(f"gainsw_{n}", [P, w]) for n, w in
                    (("ikv", 192), ("aq", 64), ("cq", 64), ("ck", 64))}
        norm_gain = whole.cut("norm_gain", [P, 4, KT])
        neg_half = whole.cut("neg_half", [P, 8])
        idx_w = whole.cut("idx_w", [P, TILES, 8])
        sinks = whole.cut("sinks", [P, 16])
        neg_sinks = whole.cut("neg_sinks", [P, 16])
        head_ss = whole.cut("head_ss", [P, 2, 8])
        head_rstd = whole.cut("head_rstd", [P, 2, 8])
        cos_g = whole.cut("cos_g", [P, 2, 192])
        sin_g = whole.cut("sin_g", [P, 2, 192])
        neg_max = whole.cut("neg_max", [P, 4, 4])
        row_sum = whole.cut("row_sum", [P, 4, 4])
        row_inv = whole.cut("row_inv", [P, 2, 4])
        raw_max = whole.cut("raw_max", [P, 4, 4])
        sink_e = whole.cut("sink_e", [P, 4, 4])
        top8 = whole.cut("top8", [P, 8])
        act_hi = whole.cut("act_hi", [P, KT, NTOK], F32R)
        act_lo = whole.cut("act_lo", [P, KT, NTOK], F32R)
        raw = whole.cut("raw", [P, 4, SW])
        ring_hi_at = whole.spans[0][0]
        ring_hi = whole.cut("ring_hi", [P, RING, SW], F32R)
        ring_lo_at = whole.spans[0][0]
        ring_lo = whole.cut("ring_lo", [P, RING, SW], F32R)
        rest_at = whole.spans[0][0]
        xt_at = (top - KT * NTOK * 4) // 64 * 64
        xT = nc.alloc_sbuf_tensor_at("xT", [P, KT, NTOK], F32, offset=xt_at)
        slot = SW * 4

        rest = Region((rest_at, xt_at))
        hT_hi, hT_lo = [None, None], [None, None]
        hT_hi[0] = nc.alloc_sbuf_tensor_at("hT_hi0", [P, 2, NTOK], F32R, offset=rest_at)
        hT_lo[0] = nc.alloc_sbuf_tensor_at("hT_lo0", [P, 2, NTOK], F32R, offset=rest_at + 8704)
        rest.spans[0][0] += 2 * 8704
        silu_out = rest.cut("silu_out", [P, 2, 384])
        hT_hi[1] = nc.alloc_sbuf_tensor_at("hT_hi1", [P, 2, NTOK], F32R, offset=rest.spans[0][0])
        sq_full = nc.alloc_sbuf_tensor_at("sq_full", [P, NTOK], F32, offset=rest.spans[0][0])
        hT_lo_1_at = ring_lo_at + 12 * slot
        hT_lo[1] = [nc.alloc_sbuf_tensor_at("hT_lo1a", [P, NTOK], F32R, offset=ring_hi_at + 12 * slot),
                    nc.alloc_sbuf_tensor_at("hT_lo1b", [P, NTOK], F32R, offset=hT_lo_1_at)]
        over = Region((rest_at, rest_at + 2 * 8704))
        n_var = over.cut("n_var", [P, NTOK])
        n_rstd = over.cut("n_rstd", [P, NTOK])
        n_tmp = over.cut("n_tmp", [P, NTOK])
        n_y = over.cut("n_y", [P, 2, 384])
        assert rest.spans[0][0] + 8704 <= xt_at

        def h_hi(par, f):
            return hT_hi[par][:, f, :]

        def h_lo(par, f):
            return hT_lo[0][:, f, :] if par == 0 else hT_lo[1][f][:, :]

        pr = Region((rest_at, xt_at))
        p_sq = pr.cut("p_sq", [P, 512])
        p_yn = pr.cut("p_yn", [P, 2, 512])
        p_rot = pr.cut("p_rot", [P, 512])
        p_out = pr.cut("p_out", [P, 3, 512])
        relu_w = pr.cut("relu_w", [P, 2, 512])
        relu_o = pr.cut("relu_o", [P, 2, 512])
        ikT = pr.cut("ikT", [P, 1600])
        xr = Region((xt_at, top))
        score = xr.cut("score", [P, SCORE_COLS])
        iqT = xr.cut("iqT", [P, len(TOPK_TILES), 4, P])
        er = Region((ring_hi_at + 4 * slot, ring_lo_at), (ring_lo_at + 4 * slot, rest_at),
                    (rest_at, xt_at), (xt_at + SCORE_COLS * 4, top))
        cr = Region((ring_hi_at + 4 * slot, ring_lo_at), (ring_lo_at + 4 * slot, rest_at),
                    (rest_at, xt_at))

        def attn_buffers(r, n, width, ktw):
            b = {}
            b["q_tok"] = r.cut(f"q_tok{n}", [P, 2, width])
            b["k_tok"] = r.cut(f"k_tok{n}", [P, 2, ktw])
            b["qT"] = r.cut(f"qT{n}", [P, 2, width])
            b["L"] = r.cut(f"L{n}", [P, 3, 1024])
            b["PT"] = r.cut(f"PT{n}", [P, 2, 1024])
            b["o_tok"] = [r.cut(f"o_tok{n}_{i}", [P, width]) for i in range(2)]
            return b

        bias = er.cut("bias", [P, 8, 640])
        v_b = er.cut("v_b", [P, 6, 512])
        kT_b = er.cut("kT_b", [P, 4, 6, P])
        v_a = er.cut("v_a", [P, 13, 128])
        kT_a = er.cut("kT_a", [P, 1600])
        eb = attn_buffers(er, 0, 512, 512)
        cb = attn_buffers(cr, 1, 1024, 128)
        kT_c = cr.cut("kT_c", [P, 10, P])
        v_c = cr.cut("v_c", [P, 10, 128])

        banks = [ctx.enter_context(nc.psum_tensor(f"bank{i}", [P, 512], F32)) for i in (4, 5, 6, 7)]
        s_banks = [ctx.enter_context(nc.psum_tensor(f"s_banks{i}", [P, 1024], F32)) for i in range(2)]

        def bank(i):
            return s_banks[i // 2][:, 512 * (i % 2):512 * (i % 2) + 512] if i < 4 else banks[i - 4][:, :]

        def sem(name):
            return ctx.enter_context(nc.semaphore(name))

        scr = {n: nc.dram_tensor(f"scratch_{n}", [TILES, P, w], F32, kind="Internal").ap()
               for n, w in (("aq", 512), ("akv", 256), ("bq", 512), ("bk", 512), ("bv", 512),
                            ("cq", 1024), ("ckv", 256))}

        const_in = sem("const_in")
        xt_in = [sem(f"xt_in{i}") for i in range(4)]
        raw_in = [sem(f"raw_in{i}") for i in range(4)]
        hi_done = sem("hi_done")
        lo_done = sem("lo_done")
        pool_init = sem("pool_init")
        dve_init = sem("dve_init")
        sq_made = sem("sq_made")
        sq_summed = sem("sq_summed")
        var_made = sem("var_made")
        root_made = sem("root_made")
        y_made = sem("y_made")
        xn_hi = sem("xn_hi")
        xn_lo = sem("xn_lo")
        unit_mm = sem("unit_mm")
        unit_sq = sem("unit_sq")
        unit_ss = sem("unit_ss")
        unit_rstd = sem("unit_rstd")
        unit_tab = sem("unit_tab")
        unit_read = sem("unit_read")
        unit_rot = sem("unit_rot")
        unit_out = sem("unit_out")
        stored = [sem(f"stored{i}") for i in range(3)]
        ixt_mm = sem("ixt_mm")
        ixt_out = sem("ixt_out")
        piece_mm = sem("piece_mm")
        piece_relu = sem("piece_relu")
        piece_w = sem("piece_w")
        piece_add = sem("piece_add")
        idxcache_in = sem("idxcache_in")
        topk_a = sem("topk_a")
        topk_b = sem("topk_b")
        mask_made = sem("mask_made")
        out_mm = sem("out_mm")
        out_add = sem("out_add")
        upf_mm = sem("upf_mm")
        silu_made = sem("silu_made")
        h_made = sem("h_made")
        h_hi_made = sem("h_hi_made")
        h_lo_made = sem("h_lo_made")
        dn_mm = sem("dn_mm")
        dn_add = sem("dn_add")
        y_out = sem("y_out")
        cache_in, bias_in, bias_made = sem("cache_in"), sem("bias_in"), sem("bias_made")
        job_in = [sem("job_in0"), sem("job_in1")]
        ccache_in = sem("ccache_in")
        cjob_in = [sem("cjob_in0"), sem("cjob_in1")]

        class AttnSems:
            def __init__(self, n):
                self.qk_mm = sem(f"qk_mm{n}")
                self.logit = sem(f"logit{n}")
                self.mx = sem(f"mx{n}")
                self.prob = sem(f"prob{n}")
                self.pt_mm = sem(f"pt_mm{n}")
                self.pt_out = sem(f"pt_out{n}")
                self.pv_mm = sem(f"pv_mm{n}")
                self.inv = sem(f"inv{n}")
                self.o_made = sem(f"o_made{n}")
                self.tr_mm = sem(f"tr_mm{n}")
                self.qk_out = sem(f"qk_out{n}")
                self.o_hi = sem(f"o_hi{n}")
                self.o_lo = sem(f"o_lo{n}")

        asem = [AttnSems(0), AttnSems(1)]

        def linear_groups(w, widths):
            out, c = [], 0
            for wd in widths:
                out.append([(w[:, k, c:c + wd], wd) for k in range(KT)])
                c += wd
            return out

        groups = (linear_groups(a["w_even"], [g[1] for g in EVEN_GROUPS]) +
                  linear_groups(a["w_out0"], [512, 512]) +
                  linear_groups(a["w_odd"], [g[1] for g in ODD_GROUPS]) +
                  linear_groups(a["w_out1"], [512, 512]))
        EVEN0, OUT0, ODD0, OUT1 = 0, 6, 8, 11
        half_of = [0, 1, 0, 1, 0, 1, 0, 1, 0, 1, 0, 1, 0]
        half_of[OUT1], half_of[OUT1 + 1] = 0, 1
        FFN_SLICES = FGROUPS * 12
        first_slice = [8 * g + (FFN_SLICES if g >= ODD0 else 0) for g in range(len(groups))]
        ffn_slice = [8 * ODD0, 8 * len(groups) + FFN_SLICES]

        def wait_group(eng, g):
            if g < OUT0:
                eng.wait_ge(unit_mm, TILES * (g + 1))
            elif ODD0 <= g < OUT1:
                eng.wait_ge(unit_mm, TILES * (OUT0 + g - ODD0 + 1))
            else:
                layer = int(g >= OUT1)
                eng.wait_ge(out_mm, 24 * layer + 12 * (g - (OUT0, OUT1)[layer] + 1))

        def group_free(eng, g):
            before = [x for x in range(g) if half_of[x] == half_of[g]]
            if before:
                wait_group(eng, before[-1])
            if g == ODD0:
                eng.wait_ge(upf_mm, 6 * FGROUPS)
            if g == ODD0 + 1:
                eng.wait_ge(dn_mm, 24 * FGROUPS)

        def load_slice(eng, i, src, width):
            if i >= 4:
                eng.wait_ge(lo_done, i - 3)
            eng.dma_start(raw[:, i % 4, 0:width], src).then_inc(raw_in[i % 4], 16)

        def split_hi(eng, i, sl, width):
            eng.wait_ge(raw_in[i % 4], 16 * (i // 4 + 1))
            eng.activation(ring_hi[:, sl, 0:width], raw[:, i % 4, 0:width], ACT.Copy).then_inc(hi_done, 1)

        def split_lo(eng, i, sl, width):
            eng.wait_ge(hi_done, i + 1)
            eng.tensor_tensor(ring_lo[:, sl, 0:width], raw[:, i % 4, 0:width],
                              ring_hi[:, sl, 0:width].bitcast(F32), ALU.subtract).then_inc(lo_done, 1)

        def group_slices(fn, eng, g, ks):
            for k in ks:
                src, width = groups[g][k]
                i = first_slice[g] + k
                if fn is load_slice:
                    load_slice(eng, i, src, width)
                else:
                    if fn is split_hi and k == 0:
                        group_free(eng, g)
                    fn(eng, i, 8 * half_of[g] + k, width)

        def proj_units(groups_of):
            return [(g, t) for g in range(len(groups_of)) for t in range(TILES)]

        UNITS = [proj_units(EVEN_GROUPS), proj_units(ODD_GROUPS)]
        UBASE = [0, len(UNITS[0])]

        def stores(layer, u):
            g, t = UNITS[layer][u]
            name = (EVEN_GROUPS, ODD_GROUPS)[layer][g][0]
            out, rows = [], slice(0, SAMPLE if t == 0 else P)
            r0 = P * (t - 1)
            if name == "ikv":
                out.append((scr["akv"][t], (64, 320), slice(0, P)))
                pre, at = ("s", slice(0, 64)) if t == 0 else ("p", slice(r0, r0 + P))
                out.append((a[pre + "a_kidx"][at, :], (0, 64), rows))
                out.append((a[pre + "a_k"][at, :], (64, 192), rows))
                out.append((a[pre + "a_v"][at, :], (192, 320), rows))
            elif name in ("aq", "bq", "bk", "bv"):
                out.append((scr[name][t], (0, 512), slice(0, P)))
                if name in ("bk", "bv") and (t == 0 or t >= 5):
                    at = slice(0, 64) if t == 0 else slice(r0 - 512, r0 - 512 + P)
                    out.append((a[("s" if t == 0 else "p") + "b_" + name[1]][at, :], (0, 512), rows))
            elif name in ("cq0", "cq1"):
                c = 512 * int(name[2])
                out.append((scr["cq"][t][:, c:c + 512], (0, 512), slice(0, P)))
            elif name == "ckv":
                out.append((scr["ckv"][t], (0, 256), slice(0, P)))
                if t in (0, 8):
                    pre = "s" if t == 0 else "p"
                    out.append((a[pre + "c_k"][:, :], (0, 128), rows))
                    out.append((a[pre + "c_v"][:, :], (128, 256), rows))
            return out

        store_count = {}
        per = [0, 0, 0]
        for _l in range(2):
            for _u in range(len(UNITS[_l])):
                per[_u % 3] += len(stores(_l, _u))
                store_count[(_l, _u)] = per[_u % 3]

        def wait_stored(eng, layer, u):
            if store_count[(layer, u)]:
                eng.wait_ge(stored[u % 3], 16 * store_count[(layer, u)])

        ALL_UNITS = [(l, u) for l in range(2) for u in range(len(UNITS[l]))]

        def spec(layer, u):
            g, t = UNITS[layer][u]
            return (EVEN_GROUPS, ODD_GROUPS)[layer][g] + (t,)

        def count_units(pred, layer, u):
            n = 0
            for l, v in ALL_UNITS:
                n += bool(pred(spec(l, v)))
                if (l, v) == (layer, u):
                    return n

        def normed(s):
            return s[2] > 0

        def rotary(s):
            return s[3] > 0

        def copied(s):
            return s[0] in ("ikv", "ckv")

        def gain_of(name):
            return {"cq0": "cq", "cq1": "cq", "ckv": "ck"}.get(name, name)

        block = ctx.enter_context(nc.Block())

        CONSTS = [(cos[:], a["cos"]), (sin[:], a["sin"]), (band_mask[:], a["band_mask"]), (c_mask[:], a["c_mask"]),
                  (ident[:], a["ident"]), (norm_gain[:], a["norm_gain"]), (sinks[:], a["sinks"])]
        CONSTS += [(gains[n][:], a[f"gain_{n}"]) for n in gains]
        CONSTS += [(gains_sw[n][:], a[f"gainsw_{n}"]) for n in gains_sw]
        plans = [EVEN_PLAN, ODD_PLAN]

        def job_loads(layer, j):
            job = plans[layer].jobs[j]
            t, b = job.t, j % 2
            if job.kind == "A":
                vb, rows = (12, 64) if t == 0 else (t - 1, P)
                return [(eb["q_tok"][:, b, :], scr["aq"][t]), (eb["k_tok"][:, b, 0:128], scr["akv"][t][:, 0:128]),
                        (v_a[0:rows, vb, :], scr["akv"][t][0:rows, 128:256])]
            if job.kind == "B":
                vb, rows = (band_block(12), 64) if t == 0 else (band_block(t - 1), P)
                return [(eb["q_tok"][:, b, :], scr["bq"][t]), (eb["k_tok"][:, b, :], scr["bk"][t]),
                        (v_b[0:rows, vb, :], scr["bv"][t][0:rows, :])]
            vb, rows = (9, 64) if t == 0 else (t - 1, P)
            return [(cb["q_tok"][:, b, :], scr["cq"][t]), (cb["k_tok"][:, b, :], scr["ckv"][t][:, 0:128]),
                    (v_c[0:rows, vb, :], scr["ckv"][t][0:rows, 128:256])]

        def job_of(jobs, kind, t):
            return next(j for j, x in enumerate(jobs) if (x.kind, x.t) == (kind, t))

        def wait_job_in(eng, layer, j):
            eng.wait_ge((job_in, cjob_in)[layer][j % 2], 48 * (j // 2 + 1))

        def load_job(eng, layer, j):
            plan, s = plans[layer], asem[layer]
            job = plan.jobs[j]
            if j >= 2:
                eng.wait_ge(s.tr_mm, plan.use_no[("k", j - 2, 0)] + 1)
            if job.kind == "B" and job.t >= 2:
                done = job_of(plan.jobs, "B", job.t - 2)
                eng.wait_ge(s.pv_mm, plan.first[done + 1])
            for dst, src in job_loads(layer, j):
                eng.dma_start(dst, src).then_inc((job_in, cjob_in)[layer][j % 2], 16)

        def load_ffn(eng, layer):
            w1, w2 = a["w_up"][layer], a["w_down"][layer]
            first = ffn_slice[layer]

            def up(g, i):
                for k in range(KT):
                    eng.wait_ge(lo_done, i + (k - 3))
                    eng.dma_start(raw[:, k % 4, :], w1[g][:, k, :]).then_inc(raw_in[k % 4], 16)

            def down(g, i):
                for k in range(4):
                    eng.wait_ge(lo_done, i + (k - 3))
                    eng.dma_start(raw[:, k % 4, :], w2[g][:, k, :]).then_inc(raw_in[k % 4], 16)

            up(0, first)
            with eng.Fori(0, (FGROUPS - 1) // 2) as it:
                for half in range(2):
                    i = it * 24 + (first + 8 + 12 * half)
                    up(it * 2 + (half + 1), i)
                    down(it * 2 + half, i + 8)
            down(FGROUPS - 1, first + 8 + 12 * (FGROUPS - 1))

        @block.sync
        def _(sp):
            for i in range(KT):
                sp.dma_start(xT[:, i, :], a["xT"][i]).then_inc(xt_in[i // 2], 16)
            for dst, src in CONSTS:
                sp.dma_start(dst, src).then_inc(const_in, 16)
            group_slices(load_slice, sp, 0, range(KT))
            sp.wait_ge(xn_lo, 24)
            for r in (0, 64):
                sp.dma_start(ikT[r:r + 64, 1024:1536], a["cache_a_kidxT"]).then_inc(idxcache_in, 16)
            for g in range(1, 6):
                group_slices(load_slice, sp, g, range(KT))
            group_slices(load_slice, sp, OUT0, range(4))
            u_last = len(UNITS[0]) - 1
            wait_group(sp, OUT0 - 1)
            sp.wait_ge(unit_out, u_last + 1)
            sp.wait_ge(piece_add, len(PIECES))
            for i in range(3):
                wait_stored(sp, 0, u_last - i)
            sp.dma_start(kT_a[:, 1024:1536], a["cache_a_kT"]).then_inc(cache_in, 16)
            sp.dma_start(v_a[:, 8:12, :], a["cache_a_v"]).then_inc(cache_in, 16)
            load_job(sp, 0, 0)
            sp.dma_start(kT_b[:, :, 0:4, :], a["cache_b_kT"]).then_inc(cache_in, 16)
            sp.dma_start(v_b[:, 0:4, :], a["cache_b_v"]).then_inc(cache_in, 16)
            sp.dma_start(bias[:], a["bias"]).then_inc(bias_in, 16)
            for j in range(1, len(EVEN_JOBS)):
                load_job(sp, 0, j)
            pl, s = EVEN_PLAN, asem[0]
            sp.wait_ge(s.o_lo, pl.count("o", pl.uses[-1]))
            sp.wait_ge(s.pv_mm, len(pl.steps))
            for i in range(KT):
                sp.dma_start(xT[:, i, :], a["xT"][i]).then_inc(xt_in[i // 2], 16)
            group_slices(load_slice, sp, OUT0, range(4, KT))
            group_slices(load_slice, sp, OUT0 + 1, range(KT))
            load_ffn(sp, 0)
            for g in range(ODD0, OUT1):
                group_slices(load_slice, sp, g, range(KT))
            group_slices(load_slice, sp, OUT1, range(4))
            u_last = len(UNITS[1]) - 1
            wait_group(sp, OUT1 - 1)
            sp.wait_ge(unit_out, UBASE[1] + u_last + 1)
            for i in range(3):
                wait_stored(sp, 1, u_last - i)
            sp.dma_start(kT_c[:, 8, :], a["cache_c_kT"]).then_inc(ccache_in, 16)
            sp.dma_start(v_c[:, 8, :], a["cache_c_v"]).then_inc(ccache_in, 16)
            for j in range(len(ODD_JOBS)):
                load_job(sp, 1, j)
            group_slices(load_slice, sp, OUT1, range(4, KT))
            group_slices(load_slice, sp, OUT1 + 1, range(KT))
            load_ffn(sp, 1)
            for n in range(KT):
                sp.wait_ge(dn_add, 24 * (2 * FGROUPS - 1) + 3 * n + 3)
                sp.dma_start(a["yT"][n], xT[:, n, :]).then_inc(y_out, 16)
            sp.wait_ge(y_out, 16 * KT)

        def mm3(pe, out, w_hi, w_lo, x_hi, x_lo, first, last):
            pe.matmul(out, w_hi, x_hi, start=first, stop=False)
            pe.matmul(out, w_hi, x_lo, start=False, stop=False)
            return pe.matmul(out, w_lo, x_hi, start=False, stop=last)

        def pe_norm_sum(pe, n, k):
            pe.wait_ge(sq_made, 8 * n + k + 1)
            if k == 0:
                if n:
                    pe.wait_ge(var_made, 6 * n)
            for c, (c0, w) in enumerate(CUTS):
                mm = pe.matmul(bank(5 + c)[:, 0:w], ones[:], sq_full[:, c0:c0 + w],
                               start=(k == 0), stop=(k == KT - 1))
            mm.then_inc(sq_summed, 1)

        def pe_index_transpose(pe, u):
            v = u - 2
            if not 0 <= v < 2 * TILES:
                return
            g, t = UNITS[0][v]
            if g == 1 and t not in TOPK_TILES:
                return
            n = ixt_no(v)
            pe.wait_ge(unit_out, v + 1)
            if n:
                pe.wait_ge(ixt_out, n)
            if g == 0:
                mm = pe.transpose(bank(3)[0:P, 0:P], ik_pair(v), ident[:])
            else:
                for i in range(4):
                    mm = pe.transpose(bank(3)[:, P * i:P * i + P], p_out[:, v % 3, P * i:P * i + P], ident[:])
            mm.then_inc(ixt_mm, 1)

        def ixt_no(v):
            return sum(1 for x in range(v) if UNITS[0][x][0] == 0 or UNITS[0][x][1] in TOPK_TILES)

        def ik_pair(v):
            return p_out[:, v % 3, 384:512]

        def pe_piece(pe, i):
            t, h, c, w, _ = PIECES[i]
            if i == 0:
                pe.wait_ge(idxcache_in, 32)
            if h == 0 and c == 0:
                pe.wait_ge(ixt_out, ixt_no(TILES + t) + 1)
            if i >= 2:
                pe.wait_ge(piece_relu, i - 1)
            r = 64 * (h % 2)
            k0 = (1024 if t == 0 else 0) + c
            pe.matmul(bank(4 + i % 2)[:, 0:w], iqT[r:r + 64, TOPK_TILES.index(t), h // 2, :],
                      ikT[r:r + 64, k0:k0 + w], start=True, stop=True).then_inc(piece_mm, 1)

        def pe_project(pe, layer, n_norm, g0):
            for u, (g, t) in enumerate(UNITS[layer]):
                width = (EVEN_GROUPS, ODD_GROUPS)[layer][g][1]
                c0, c1 = tile_cols(t)
                uu = UBASE[layer] + u
                if g == 0:
                    pe.wait_ge(xn_lo, 24 * n_norm + 8 * cuts_for(c1))
                if uu >= 3:
                    pe.wait_ge(unit_read, uu - 2)
                out = bank(uu % 3)[:, 0:width]
                for k in range(KT):
                    if t == 0:
                        pe.wait_ge(lo_done, first_slice[g0 + g] + k + 1)
                    sl = 8 * half_of[g0 + g] + k
                    pe.matmul(out, act_hi[:, k, c0:c1], ring_hi[:, sl, 0:width], start=(k == 0), stop=False)
                    pe.matmul(out, act_lo[:, k, c0:c1], ring_hi[:, sl, 0:width], start=False, stop=False)
                    mm = pe.matmul(out, act_hi[:, k, c0:c1], ring_lo[:, sl, 0:width], start=False,
                                   stop=(k == KT - 1))
                mm.then_inc(unit_mm, 1)
                if layer == 0:
                    pe_index_transpose(pe, u)
                    for i in range(pieces_by(u - 1), pieces_by(u)):
                        pe_piece(pe, i)

        def key_ops(layer, job, head, b):
            blk = job.blocks[b]
            last_sample = job.t == 0 and b == len(job.blocks) - 1
            rows = SAMPLE if last_sample else P
            if job.kind == "A":
                r, kv = 64 * (head // 4), head // 4
                return kT_a[r:r + 64, P * blk:P * blk + rows], v_a[0:rows, blk, 64 * kv:64 * kv + 64], rows
            if job.kind == "B":
                r, sl = 64 * (head % 2), band_block(blk)
                return kT_b[r:r + 64, head // 2, sl, 0:rows], v_b[0:rows, sl, 64 * head:64 * head + 64], rows
            r, kv = 64 * (head // 8), head // 8
            return kT_c[r:r + 64, blk, 0:rows], v_c[0:rows, blk, 64 * kv:64 * kv + 64], rows

        def q_pair(job, head):
            if job.kind == "A":
                return head % 4, head // 4
            if job.kind == "B":
                return head // 2, head % 2
            return head % 8, head // 8

        def step_heads(job, i):
            return list(range(job.group * i, job.group * i + job.group))

        def stride_of(job):
            return 256 if job.kind == "C" else 0

        def pe_attention(pe, layer):
            plan, s, b_ = plans[layer], asem[layer], (eb, cb)[layer]
            n_steps = len(plan.steps)

            def transposes(use):
                what, j, i = use
                job, n = plan.jobs[j], plan.use_no[use]
                if n:
                    before = plan.uses[n - 1]
                    if before[0] == "o":
                        pe.wait_ge(s.o_lo, plan.count("o", before))
                    else:
                        pe.wait_ge(s.qk_out, plan.count("qk", before))
                if what == "o":
                    pe.wait_ge(s.o_made, plan.first[j + 1])
                    src, cols = b_["o_tok"][j % 2][:, :], range(512 * i, 512 * i + 512, P)
                elif what == "q":
                    wait_job_in(pe, layer, j)
                    src, cols = b_["q_tok"][:, j % 2, :], range(512 * i, 512 * i + 512, P)
                else:
                    src, cols = b_["k_tok"][:, j % 2, :], range(0, 512 if job.kind == "B" else 128, P)
                for m, c in enumerate(cols):
                    mm = pe.transpose(bank(7)[:, P * m:P * m + P], src[:, c:c + P], ident[:])
                mm.then_inc(s.tr_mm, 1)

            def logits(n):
                j, i = plan.steps[n]
                job = plan.jobs[j]
                if i == 0:
                    pe.wait_ge(s.qk_out, plan.count("qk", ("k", j, 0)))
                if n == 0:
                    pe.wait_ge((cache_in, ccache_in)[layer], 64 if layer == 0 else 32)
                if n >= 2:
                    pe.wait_ge(s.logit, n - 1)
                for x, head in enumerate(step_heads(job, i)):
                    pair, half = q_pair(job, head)
                    q = b_["qT"][64 * half:64 * half + 64, j % 2, P * pair:P * pair + P]
                    for b in range(len(job.blocks)):
                        kT, _, rows = key_ops(layer, job, head, b)
                        c = stride_of(job) * x + P * b
                        mm = pe.matmul(s_banks[n % 2][:, c:c + rows], q, kT, start=True, stop=True)
                mm.then_inc(s.qk_mm, 1)

            def transpose_probs(n):
                j, i = plan.steps[n]
                job = plan.jobs[j]
                pe.wait_ge(s.prob, n + 1)
                for x, group in enumerate(plan.pt_groups[n]):
                    no = plan.pt_base[n] + x
                    if no >= 2:
                        pe.wait_ge(s.pt_out, no - 1)
                    for m, (g, b) in enumerate(group):
                        c = stride_of(job) * g + P * b
                        mm = pe.transpose(bank(4 + no % 2)[:, P * m:P * m + P], b_["L"][:, n % 3, c:c + P], ident[:])
                    mm.then_inc(s.pt_mm, 1)

            def times_values(n):
                j, i = plan.steps[n]
                job = plan.jobs[j]
                pe.wait_ge(s.pt_out, plan.pt_base[n + 1])
                if i == 0:
                    wait_job_in(pe, layer, j)
                if n:
                    pe.wait_ge(s.o_made, n)
                nb = len(job.blocks)
                for x, head in enumerate(step_heads(job, i)):
                    for b in range(nb):
                        _, v, rows = key_ops(layer, job, head, b)
                        c = P * (x * nb + b)
                        mm = pe.matmul(bank(6)[:, 64 * x:64 * x + 64], b_["PT"][0:rows, n % 2, c:c + P], v,
                                       start=(b == 0), stop=(b == nb - 1))
                mm.then_inc(s.pv_mm, 1)

            pe.wait_ge(unit_read, UBASE[layer] + len(UNITS[layer]))
            if layer == 0:
                pe.wait_ge(piece_relu, len(PIECES))
                pe.wait_ge(ixt_out, ixt_no(2 * TILES))
            for use in plan.at_slot(-1):
                transposes(use)
            for n in range(n_steps + 4):
                if n < n_steps:
                    logits(n)
                if 0 <= n - 1 < n_steps:
                    transpose_probs(n - 1)
                if 0 <= n - 2 < n_steps:
                    times_values(n - 2)
                for use in plan.at_slot(n):
                    transposes(use)

        def pe_out_project(pe, layer, g0, n_norm):
            plan, s = plans[layer], asem[layer]
            pe.wait_ge(s.o_lo, plan.count("o", plan.uses[-1]))
            for hf in range(2):
                for nn in range(4):
                    for c, (c0, w) in enumerate(CUTS):
                        v = 12 * hf + 3 * nn + c
                        if v >= 4:
                            pe.wait_ge(out_add, 24 * layer + v - 3)
                        for k in range(KT):
                            if nn == 0 and c == 0:
                                pe.wait_ge(lo_done, first_slice[g0 + hf] + k + 1)
                            sl = 8 * half_of[g0 + hf] + k
                            mm = mm3(pe, bank(v % 4)[:, 0:w], ring_hi[:, sl, P * nn:P * nn + P],
                                     ring_lo[:, sl, P * nn:P * nn + P], act_hi[:, k, c0:c0 + w],
                                     act_lo[:, k, c0:c0 + w], k == 0, k == KT - 1)
                        mm.then_inc(out_mm, 1)
                    if hf or nn:
                        pe_norm_sum(pe, n_norm, 4 * hf + nn - 1)
            pe_norm_sum(pe, n_norm, KT - 1)

        def pe_ffn(pe, layer, n_norm):
            first = ffn_slice[layer]
            ub, hb, db = 6 * FGROUPS * layer, 6 * FGROUPS * layer, 24 * FGROUPS * layer

            def up(par, n, i, peeled):
                for f in range(2):
                    for c, (c0, w) in enumerate(CUTS):
                        q = 3 * f + c
                        if peeled and f == 0:
                            pe.wait_ge(xn_lo, 24 * n_norm + 8 * (c + 1))
                        if not (peeled and layer == 0 and q < 2):
                            pe.wait_ge(h_made, n + (q - 1))
                        for part in range(2):
                            out = bank(2 * (q % 2) + part)[:, 0:w]
                            for k in range(KT):
                                if q == 0 and part == 0:
                                    pe.wait_ge(lo_done, i + (k + 1))
                                col = 256 * part + P * f
                                mm = mm3(pe, out, ring_hi[:, k, col:col + P], ring_lo[:, k, col:col + P],
                                         act_hi[:, k, c0:c0 + w], act_lo[:, k, c0:c0 + w], k == 0, k == KT - 1)
                        mm.then_inc(upf_mm, 1)

            def down(par, n, i, d, last):
                pe.wait_ge(h_lo_made, n)
                for m in range(KT):
                    for c, (c0, w) in enumerate(CUTS):
                        v = 3 * m + c
                        pe.wait_ge(dn_add, d + (v - 3 if v >= 4 else 0))
                        out = bank(v % 4 if last else 4 + v % 4)[:, 0:w]
                        for f in range(2):
                            if m in (0, 4) and c == 0:
                                pe.wait_ge(lo_done, i + (2 * f + m // 4 + 1))
                            sl = 8 + 2 * f + m // 4
                            col = P * (m % 4)
                            mm = mm3(pe, out, ring_hi[:, sl, col:col + P], ring_lo[:, sl, col:col + P],
                                     h_hi(par, f)[:, c0:c0 + w], h_lo(par, f)[:, c0:c0 + w], f == 0, f == 1)
                        mm.then_inc(dn_mm, 1)
                    if last and layer == 0 and m:
                        pe_norm_sum(pe, 2, m - 1)
                if last and layer == 0:
                    pe_norm_sum(pe, 2, KT - 1)

            up(0, ub, first, True)
            with pe.Fori(0, (FGROUPS - 1) // 2) as it:
                for half in range(2):
                    i = it * 24 + (first + 8 + 12 * half)
                    n = it * 12 + (ub + 6 * (half + 1))
                    up((half + 1) % 2, n, i, False)
                    down(half, n, i + 8, it * 48 + (db + 24 * half), False)
            down(0, ub + 6 * FGROUPS, first + 8 + 12 * (FGROUPS - 1), db + 24 * (FGROUPS - 1), True)

        @block.tensor
        def _(pe):
            pe.wait_ge(const_in, 16 * len(CONSTS))
            pe.wait_ge(dve_init, 1)
            for k in range(KT):
                pe_norm_sum(pe, 0, k)
            pe_project(pe, 0, 0, EVEN0)
            pe_attention(pe, 0)
            pe_out_project(pe, 0, OUT0, 1)
            pe_ffn(pe, 0, 1)
            pe_project(pe, 1, 2, ODD0)
            pe_attention(pe, 1)
            pe_out_project(pe, 1, OUT1, 3)
            pe_ffn(pe, 1, 3)

        def act_norm_square(act, n, k, wait):
            wait(k)
            if k:
                act.wait_ge(sq_summed, 8 * n + k)
            act.activation(sq_full[:], xT[:, k, :], ACT.Square).then_inc(sq_made, 1)

        def act_norm_rest(act, n):
            act.wait_ge(var_made, 6 * n + 1)
            act.activation(n_tmp[:], n_var[:], ACT.Sqrt).then_inc(root_made, 1)
            for c, (c0, w) in enumerate(CUTS):
                for k in range(KT):
                    q = 8 * c + k
                    act.wait_ge(y_made, 24 * n + q + 1)
                    act.activation(act_hi[:, k, c0:c0 + w], n_y[:, q % 2, 0:w], ACT.Copy).then_inc(xn_hi, 1)

        def act_store(act, layer, v):
            if 0 <= v < len(UNITS[layer]):
                act.wait_ge(unit_out, UBASE[layer] + v + 1)
                for dst, (c0, c1), rows in stores(layer, v):
                    act.dma_start(dst, p_out[rows, v % 3, c0:c1]).then_inc(stored[v % 3], 16)

        def act_project(act, layer, g0):
            n_groups = len((EVEN_GROUPS, ODD_GROUPS)[layer])
            for u, (g, t) in enumerate(UNITS[layer]):
                name, width, nh, nr, _ = spec(layer, u)
                uu = UBASE[layer] + u
                act_store(act, layer, u - 2)
                if nh:
                    act.wait_ge(unit_mm, uu + 1)
                    n = count_units(normed, layer, u)
                    if n > 1:
                        act.wait_ge(unit_ss, n - 1)
                    sq = act.activation(p_sq[:, 0:64 * nh], bank(uu % 3)[:, 0:64 * nh], ACT.Square)
                    if copied((name,)):
                        if u >= 3:
                            wait_stored(act, layer, u - 3)
                        if name == "ikv" and u >= 3:
                            act.wait_ge(ixt_mm, u - 2)
                        c0 = 64 * nh
                        sq = act.activation(p_out[:, u % 3, c0:c0 + 128], bank(uu % 3)[:, c0:c0 + 128], ACT.Copy)
                        if name == "ikv":
                            sq = act.activation(idx_w[:, t, :], bank(uu % 3)[:, 320:328], ACT.Copy, scale=IDX_SCALE)
                    sq.then_inc(unit_sq, 1)
                if t < KT and g + 1 < n_groups:
                    group_slices(split_hi, act, g0 + g + 1, [t])
                if layer == 0:
                    v = u - 2
                    if 0 <= v < 2 * TILES and (UNITS[0][v][0] == 0 or UNITS[0][v][1] in TOPK_TILES):
                        act.wait_ge(ixt_mm, ixt_no(v) + 1)
                        gg, tt = UNITS[0][v]
                        if gg == 0:
                            dst = ikT[:, 1536:1600] if tt == 0 else ikT[:, P * (tt - 1):P * tt]
                            src = bank(3)[:, 0:SAMPLE if tt == 0 else P]
                        else:
                            dst, src = iqT[:, TOPK_TILES.index(tt), :, :].rearrange("p a b -> p (a b)"), bank(3)
                        act.activation(dst, src, ACT.Copy).then_inc(ixt_out, 1)
                    for i in range(pieces_by(u - 1), pieces_by(u)):
                        tt, h, c, w, _ = PIECES[i]
                        act.wait_ge(piece_mm, i + 1)
                        if i >= 2:
                            act.wait_ge(piece_w, i - 1)
                        act.activation(relu_o[:, i % 2, 0:w], bank(4 + i % 2)[:, 0:w], ACT.Relu).then_inc(piece_relu, 1)
                        act.wait_ge(piece_relu, i + 1)
                        if i >= 2:
                            act.wait_ge(piece_add, i - 1)
                        act.activation(relu_w[:, i % 2, 0:w], relu_o[:, i % 2, 0:w], ACT.Copy,
                                       scale=idx_w[:, tt, h:h + 1]).then_inc(piece_w, 1)
            act_store(act, layer, len(UNITS[layer]) - 2)
            act_store(act, layer, len(UNITS[layer]) - 1)

        def act_attention(act, layer):
            plan, s, b_ = plans[layer], asem[layer], (eb, cb)[layer]
            n_steps = len(plan.steps)

            def bank7(use):
                what, j, i = use
                job, n = plan.jobs[j], plan.use_no[use]
                act.wait_ge(s.tr_mm, n + 1)
                if what == "o":
                    c0, c1 = tile_cols(job.t)
                    if job.t == 0:
                        c1 = SAMPLE
                    k0 = 4 if job.kind == "B" else 4 * i
                    src = bank(7).rearrange("p (a b) -> p a b", a=4)[:, :, 0:c1 - c0]
                    act.activation(act_hi[:, k0:k0 + 4, c0:c1], src, ACT.Copy).then_inc(s.o_hi, 1)
                    return
                if what == "q":
                    if j >= 2:
                        act.wait_ge(s.qk_mm, plan.first[j - 1])
                    act.activation(b_["qT"][:, j % 2, 512 * i:512 * i + 512], bank(7), ACT.Copy).then_inc(s.qk_out, 1)
                    return
                cols = SAMPLE if job.t == 0 else P
                if job.kind == "B":
                    if job.t >= 2:
                        act.wait_ge(s.qk_mm, plan.first[job_of(plan.jobs, "B", job.t - 2) + 1])
                    dst = kT_b[:, :, band_block(12 if job.t == 0 else job.t - 1), 0:cols]
                    src = bank(7).rearrange("p (a b) -> p a b", a=4)[:, :, 0:cols]
                elif job.kind == "A":
                    b = 12 if job.t == 0 else job.t - 1
                    dst, src = kT_a[:, P * b:P * b + cols], bank(7)[:, 0:cols]
                else:
                    dst, src = kT_c[:, 9 if job.t == 0 else job.t - 1, 0:cols], bank(7)[:, 0:cols]
                act.activation(dst, src, ACT.Copy).then_inc(s.qk_out, 1)

            for use in plan.at_slot(-1):
                bank7(use)
            for n in range(n_steps + 4):
                if 0 <= n - 1 < n_steps:
                    m = n - 1
                    for x, group in enumerate(plan.pt_groups[m]):
                        no = plan.pt_base[m] + x
                        act.wait_ge(s.pt_mm, no + 1)
                        if x == 0 and m >= 2:
                            act.wait_ge(s.pv_mm, m - 1)
                        w = P * len(group)
                        act.activation(b_["PT"][:, m % 2, 512 * x:512 * x + w], bank(4 + no % 2)[:, 0:w],
                                       ACT.Copy).then_inc(s.pt_out, 1)
                if n < n_steps:
                    j, i = plan.steps[n]
                    job, w = plan.jobs[j], plan.jobs[j].width
                    if job.kind == "C":
                        act.wait_ge(s.mx, 2 * n + 2)
                        for x in range(4):
                            L = b_["L"][:, n % 3, 256 * x:256 * x + w]
                            act.activation(L, L, ACT.Exp, bias=neg_max[:, n % 4, x:x + 1], scale=HD ** -0.5,
                                           accum_out=row_sum[:, n % 4, x:x + 1])
                        act.activation(sink_e[:, n % 4, :], raw_max[:, n % 4, :], ACT.Exp).then_inc(s.prob, 1)
                    else:
                        act.wait_ge(s.logit, n + 1)
                        L = b_["L"][:, n % 3, 0:w]
                        act.activation(L, L, ACT.Exp, bias=neg_max[:, n % 4, 0:1], scale=-1.0,
                                       accum_out=row_sum[:, n % 4, 0:1]).then_inc(s.prob, 1)
                for use in plan.at_slot(n):
                    bank7(use)

        def act_out_project(act, layer, g0, n_norm):
            pl, s = plans[layer], asem[layer]
            act.wait_ge(s.pv_mm, len(pl.steps))
            act.wait_ge(s.o_lo, pl.count("o", pl.uses[-1]))
            group_slices(split_hi, act, g0, range(4, KT))
            group_slices(split_hi, act, g0 + 1, range(KT))

            def wait(k):
                act.wait_ge(out_add, 24 * layer + 3 * k + 3)

            for k in range(KT):
                if k == 4:
                    wait_group(act, g0)
                    ffn_hi(act, ffn_slice[layer], 0, 8)
                act_norm_square(act, n_norm, k, wait)

        def ffn_hi(act, i0, sl, n):
            for k in range(n):
                act.wait_ge(raw_in[k % 4], i0 * 4 + 16 * (k // 4 + 1))
                act.activation(ring_hi[:, sl + k, :], raw[:, k % 4, :], ACT.Copy).then_inc(hi_done, 1)

        def act_ffn(act, layer):
            first = ffn_slice[layer]
            ub, db = 6 * FGROUPS * layer, 24 * FGROUPS * layer

            def pieces(par, n, fresh=False):
                for q in range(6):
                    f, c = divmod(q, 3)
                    c0, w = CUTS[c]
                    act.wait_ge(upf_mm, n + (q + 1))
                    if not fresh or q >= 2:
                        act.wait_ge(h_lo_made, n + (q - 1))
                    act.activation(silu_out[:, q % 2, 0:w], bank(2 * (q % 2))[:, 0:w], ACT.Silu).then_inc(silu_made, 1)
                    act.wait_ge(h_made, n + (q + 1))
                    act.activation(h_hi(par, f)[:, c0:c0 + w], silu_out[:, q % 2, 0:w], ACT.Copy).then_inc(h_hi_made, 1)

            wait_group(act, (OUT0, OUT1)[layer] + 1)
            pieces(0, ub, fresh=(layer == 0))
            with act.Fori(0, (FGROUPS - 1) // 2) as it:
                for half in range(2):
                    i = it * 24 + (first + 8 + 12 * half)
                    act.wait_ge(upf_mm, it * 12 + (ub + 6 * (half + 1)))
                    ffn_hi(act, i, 0, 8)
                    act.wait_ge(dn_mm, it * 48 + (db + 24 * half))
                    ffn_hi(act, i + 8, 8, 4)
                    pieces((half + 1) % 2, it * 12 + (ub + 6 * (half + 1)))
            act.wait_ge(dn_mm, db + 24 * (FGROUPS - 1))
            ffn_hi(act, first + 8 + 12 * (FGROUPS - 1), 8, 4)
            if layer == 0:
                group_slices(split_hi, act, ODD0, range(KT))
                for k in range(KT):
                    act_norm_square(act, 2, k, lambda k: act.wait_ge(dn_add, 24 * (FGROUPS - 1) + 3 * k + 3))

        @block.scalar
        def _(act):
            for k in range(KT):
                act_norm_square(act, 0, k, lambda k: act.wait_ge(xt_in[k // 2], 32))
            group_slices(split_hi, act, 0, range(KT))
            act_norm_rest(act, 0)
            act.wait_ge(xn_lo, 24)
            act.wait_ge(pool_init, 1)
            act_project(act, 0, EVEN0)
            group_slices(split_hi, act, OUT0, range(4))
            wait_group(act, OUT0 - 1)
            act.wait_ge(piece_add, len(PIECES))
            act.wait_ge(unit_out, len(UNITS[0]))
            for i in range(3):
                wait_stored(act, 0, len(UNITS[0]) - 1 - i)
            act_attention(act, 0)
            act_out_project(act, 0, OUT0, 1)
            act_norm_rest(act, 1)
            act_ffn(act, 0)
            act_norm_rest(act, 2)
            act.wait_ge(xn_lo, 72)
            act_project(act, 1, ODD0)
            group_slices(split_hi, act, OUT1, range(4))
            wait_group(act, OUT1 - 1)
            act.wait_ge(unit_out, UBASE[1] + len(UNITS[1]))
            for i in range(3):
                wait_stored(act, 1, len(UNITS[1]) - 1 - i)
            act_attention(act, 1)
            act_out_project(act, 1, OUT1, 3)
            act_norm_rest(act, 3)
            act_ffn(act, 1)

        def pool_project(pool, layer, g0):
            n_groups = len((EVEN_GROUPS, ODD_GROUPS)[layer])

            def tables(u):
                name, width, nh, nr, t = spec(layer, u)
                if not nr:
                    return
                n = count_units(rotary, layer, u)
                if n > 2:
                    pool.wait_ge(unit_rot, 2 * (n - 2))
                b = n % 2
                if nh == 0:
                    pool.tensor_copy(cos_g[:, b, 0:HD], cos[:, t, :])
                    pool.tensor_copy(sin_g[:, b, 0:HD], sin[:, t, :]).then_inc(unit_tab, 1)
                    return
                gw = 192 if name == "ikv" else 64
                r = gw // 64
                for dst, src, gn in ((cos_g, cos, gains), (sin_g, sin, gains_sw)):
                    ins = pool.tensor_tensor(
                        dst[:, b, 0:gw].rearrange("p (h d) -> p h d", h=r),
                        src[:, t, :].rearrange("p (o d) -> p o d", o=1).to_broadcast([P, r, HD]),
                        gn[gain_of(name)][:, 0:gw].rearrange("p (h d) -> p h d", h=r), ALU.mult)
                ins.then_inc(unit_tab, 1)

            def rstd(u):
                name, width, nh, nr, t = spec(layer, u)
                if not nh:
                    return
                n = count_units(normed, layer, u)
                pool.wait_ge(unit_ss, n)
                b = n % 2
                if n > 2:
                    pool.wait_ge(unit_read, [UBASE[l] + v for l, v in ALL_UNITS if normed(spec(l, v))][n - 3] + 1)
                pool.tensor_scalar(head_rstd[:, b, 0:nh], head_ss[:, b, 0:nh], 1.0 / HD, EPS,
                                   ALU.mult, ALU.add).then_inc(unit_rstd, 1)
                pool.wait_ge(unit_rstd, 2 * n - 1)
                pool.tensor_tensor(head_rstd[:, b, 0:nh], head_rstd[:, b, 0:nh], neg_half[:, 0:nh],
                                   ALU.pow).then_inc(unit_rstd, 1)

            tables(0)
            for u, (g, t) in enumerate(UNITS[layer]):
                rstd(u)
                if u + 1 < len(UNITS[layer]):
                    tables(u + 1)
                if t < KT and g + 1 < n_groups:
                    group_slices(split_lo, pool, g0 + g + 1, [t])
                if layer == 0:
                    for i in range(pieces_by(u - 1), pieces_by(u)):
                        tt, h, c, w, _ = PIECES[i]
                        pool.wait_ge(piece_w, i + 1)
                        if i:
                            pool.wait_ge(piece_add, i)
                        o = SCORE_OFF[tt] + c
                        pool.tensor_tensor(score[:, o:o + w], score[:, o:o + w], relu_w[:, i % 2, 0:w],
                                           ALU.add).then_inc(piece_add, 1)

        def pool_ffn(pool, layer):
            first = ffn_slice[layer]

            def lo(i0, sl, n):
                for k in range(n):
                    pool.wait_ge(hi_done, i0 + (k + 1))
                    pool.tensor_tensor(ring_lo[:, sl + k, :], raw[:, k % 4, :],
                                       ring_hi[:, sl + k, :].bitcast(F32), ALU.subtract).then_inc(lo_done, 1)

            lo(first, 0, 8)
            with pool.Fori(0, (FGROUPS - 1) // 2) as it:
                for half in range(2):
                    i = it * 24 + (first + 8 + 12 * half)
                    lo(i, 0, 8)
                    lo(i + 8, 8, 4)
            lo(first + 8 + 12 * (FGROUPS - 1), 8, 4)

        @block.gpsimd
        def _(pool):
            pool.memset(neg_half[:], -0.5)
            pool.wait_ge(const_in, 16 * len(CONSTS))
            group_slices(split_lo, pool, 0, range(KT))
            pool.wait_ge(xn_lo, 24)
            pool.memset(score[:], 0.0).then_inc(pool_init, 1)
            pool.wait_ge(pool_init, 1)
            for t in TOPK_TILES[1:]:
                o = SCORE_OFF[t] + score_width(t) - P
                ins = pool.tensor_copy(score[:, o:o + P], band_mask[:, 512:640])
            ins.then_inc(pool_init, 1)
            pool.wait_ge(pool_init, 2)
            pool_project(pool, 0, EVEN0)
            group_slices(split_lo, pool, OUT0, range(4))
            group_slices(split_lo, pool, OUT0, range(4, KT))
            group_slices(split_lo, pool, OUT0 + 1, range(KT))
            pool_ffn(pool, 0)
            group_slices(split_lo, pool, ODD0, range(KT))
            pool.wait_ge(xn_lo, 72)
            pool_project(pool, 1, ODD0)
            group_slices(split_lo, pool, OUT1, range(KT))
            group_slices(split_lo, pool, OUT1 + 1, range(KT))
            pool_ffn(pool, 1)

        def dve_norm_rest(dve, n):
            dve.wait_ge(sq_summed, 8 * n + 8)
            for c, (c0, w) in enumerate(CUTS):
                ins = dve.tensor_scalar(n_var[:, c0:c0 + w], bank(5 + c)[:, 0:w], 1.0 / D, EPS, ALU.mult, ALU.add)
            ins.then_inc(var_made, 1)
            dve.wait_ge(root_made, n + 1)
            dve.reciprocal(n_rstd[:], n_tmp[:]).then_inc(var_made, 1)
            dve.wait_ge(var_made, 6 * n + 2)
            dve.tensor_tensor(n_tmp[:], n_rstd[:], n_rstd[:], ALU.mult).then_inc(var_made, 1)
            dve.wait_ge(var_made, 6 * n + 3)
            dve.tensor_tensor(n_tmp[:], n_tmp[:], n_var[:], ALU.mult).then_inc(var_made, 1)
            dve.wait_ge(var_made, 6 * n + 4)
            dve.tensor_scalar(n_tmp[:], n_tmp[:], -0.5, 1.5, ALU.mult, ALU.add).then_inc(var_made, 1)
            dve.wait_ge(var_made, 6 * n + 5)
            dve.tensor_tensor(n_rstd[:], n_rstd[:], n_tmp[:], ALU.mult).then_inc(var_made, 1)
            dve.wait_ge(var_made, 6 * n + 6)

            def y(q):
                c, k = divmod(q, 8)
                c0, w = CUTS[c]
                dve.scalar_tensor_tensor(n_y[:, q % 2, 0:w], xT[:, k, c0:c0 + w], norm_gain[:, n, k:k + 1],
                                         n_rstd[:, c0:c0 + w], ALU.mult, ALU.mult).then_inc(y_made, 1)

            def lo(q):
                c, k = divmod(q, 8)
                c0, w = CUTS[c]
                dve.wait_ge(xn_hi, 24 * n + q + 1)
                dve.tensor_tensor(act_lo[:, k, c0:c0 + w], n_y[:, q % 2, 0:w],
                                  act_hi[:, k, c0:c0 + w].bitcast(F32), ALU.subtract).then_inc(xn_lo, 1)
            for q in range(24):
                if q >= 2:
                    dve.wait_ge(xn_lo, 24 * n + q - 1)
                y(q)
                if q:
                    lo(q - 1)
            lo(23)

        def topk_round(dve, r):
            t, last = ROUNDS[r]
            first = r == 0 or ROUNDS[r - 1][0] != t
            sc = score[:, SCORE_OFF[t]:SCORE_OFF[t] + score_width(t)]
            if first:
                dve.wait_ge(piece_add, PIECE_END[t])
            if r:
                dve.wait_ge(topk_b, r)
            dve.max(top8[:], sc).then_inc(topk_a, 1)
            dve.wait_ge(topk_a, r + 1)
            dve.match_replace(sc, top8[:], sc, TAKEN).then_inc(topk_b, 1)
            if last:
                dve.wait_ge(topk_b, r + 1)
                dve.tensor_scalar(sc, sc, TAKEN / 2, MASKED, ALU.is_gt, ALU.mult).then_inc(mask_made, 1)

        def dve_project(dve, layer):
            n_units = len(UNITS[layer])

            def sums(u):
                name, width, nh, nr, t = spec(layer, u)
                if nh:
                    n = count_units(normed, layer, u)
                    dve.wait_ge(unit_sq, n)
                    dve.tensor_reduce(head_ss[:, n % 2, 0:nh], p_sq[:, 0:64 * nh].rearrange("p (h d) -> p h d", h=nh),
                                      AX.X, ALU.add).then_inc(unit_ss, 1)

            def finish(u):
                name, width, nh, nr, t = spec(layer, u)
                uu, ps = UBASE[layer] + u, bank((UBASE[layer] + u) % 3)
                hn = max(nh, nr)
                cols = 64 * hn if hn else width
                if u >= 3:
                    wait_stored(dve, layer, u - 3)
                    if layer == 0 and u - 3 < 2 * TILES:
                        dve.wait_ge(ixt_mm, ixt_no(u - 2))
                out = p_out[:, u % 3, 0:cols]
                yn = p_yn[:, u % 2, 0:cols]

                def heads(x):
                    return x.rearrange("p (h d) -> p h d", h=hn)

                dve.wait_ge(unit_mm, uu + 1)
                if nh:
                    n = count_units(normed, layer, u)
                    dve.wait_ge(unit_rstd, 2 * n)
                    dve.wait_ge(unit_sq, n)
                    r = head_rstd[:, n % 2, 0:hn].rearrange("p (h o) -> p h o", o=1).to_broadcast([P, hn, HD])
                    dve.tensor_tensor(heads(yn), heads(ps[:, 0:cols]), r, ALU.mult).then_inc(unit_read, 1)
                elif nr:
                    dve.tensor_copy(yn, ps[:, 0:cols]).then_inc(unit_read, 1)
                else:
                    dve.tensor_copy(out, ps[:, 0:cols]).then_inc(unit_read, 1)
                    dve.wait_ge(unit_read, uu + 1)
                    dve.engine_nop().then_inc(unit_out, 1)
                    return
                dve.wait_ge(unit_read, uu + 1)
                if not nr:
                    g = gains[gain_of(name)][:, 0:64].rearrange("p (o d) -> p o d", o=1).to_broadcast([P, hn, HD])
                    dve.tensor_tensor(heads(out), heads(yn), g, ALU.mult).then_inc(unit_out, 1)
                    return
                n = count_units(rotary, layer, u)
                dve.wait_ge(unit_tab, n)
                if name == "ikv":
                    c_, s_ = heads(cos_g[:, n % 2, 0:192]), heads(sin_g[:, n % 2, 0:192])
                else:
                    c_, s_ = [x[:, n % 2, 0:HD].rearrange("p (o d) -> p o d", o=1).to_broadcast([P, hn, HD])
                              for x in (cos_g, sin_g)]
                dve.tensor_tensor(heads(out), heads(yn), c_, ALU.mult)
                y2, r2 = heads(yn), heads(p_rot[:, 0:cols])
                dve.tensor_tensor(r2[:, :, 0:32], y2[:, :, 32:64], s_[:, :, 0:32], ALU.mult).then_inc(unit_rot, 1)
                dve.tensor_tensor(r2[:, :, 32:64], y2[:, :, 0:32], s_[:, :, 32:64], ALU.mult).then_inc(unit_rot, 1)
                dve.wait_ge(unit_rot, 2 * n)
                ins = dve.tensor_tensor(out, out, p_rot[:, 0:cols], ALU.add)
                if name == "ikv":
                    ins.then_inc(unit_rot2, 1)
                    dve.wait_ge(unit_rot2, u + 1)
                    dve.tensor_copy(p_out[:, u % 3, 384:448], p_out[:, u % 3, 0:64])
                    ins = dve.tensor_copy(p_out[:, u % 3, 448:512], p_out[:, u % 3, 0:64])
                ins.then_inc(unit_out, 1)

            for u in range(n_units):
                sums(u)
                if u:
                    finish(u - 1)
                if layer == 0:
                    for r in range(rounds_by_unit(u - 1), rounds_by_unit(u)):
                        topk_round(dve, r)
            finish(n_units - 1)

        unit_rot2 = sem("unit_rot2")

        def dve_attention(dve, layer):
            plan, s, b_ = plans[layer], asem[layer], (eb, cb)[layer]
            n_steps = len(plan.steps)
            done = rounds_by_unit(len(UNITS[0]) - 1)

            def scale_out(m):
                j, i = plan.steps[m]
                job = plan.jobs[j]
                g = job.group
                rs = row_sum[:, m % 4, 0:g]
                dve.wait_ge(s.pv_mm, m + 1)
                dve.wait_ge(s.prob, m + 1)
                if job.kind == "C":
                    dve.tensor_tensor(rs, rs, sink_e[:, m % 4, :], ALU.add).then_inc(s.inv, 1)
                    dve.wait_ge(s.inv, 2 * m + 1)
                dve.reciprocal(row_inv[:, m % 2, 0:g], rs).then_inc(s.inv, 1)
                dve.wait_ge(s.inv, (2 if job.kind == "C" else 1) * (m + 1))
                if i == 0 and j >= 2:
                    dve.wait_ge(s.tr_mm, plan.use_no[plan.bank_uses(j - 2, "o")[-1]] + 1)
                out = b_["o_tok"][j % 2][:, 64 * g * i:64 * g * (i + 1)]
                if g == 1:
                    dve.tensor_scalar(out, bank(6)[:, 0:64], row_inv[:, m % 2, 0:1], None, ALU.mult).then_inc(s.o_made, 1)
                else:
                    r = row_inv[:, m % 2, 0:g].rearrange("p (h o) -> p h o", o=1).to_broadcast([P, g, HD])
                    dve.tensor_tensor(out.rearrange("p (h d) -> p h d", h=g),
                                      bank(6)[:, 0:64 * g].rearrange("p (h d) -> p h d", h=g), r,
                                      ALU.mult).then_inc(s.o_made, 1)

            def mask_logits(n):
                j, i = plan.steps[n]
                job, w = plan.jobs[j], plan.jobs[j].width
                dve.wait_ge(s.qk_mm, n + 1)
                if n >= 3:
                    dve.wait_ge(s.pt_mm, plan.pt_base[n - 2])
                first_col = 0 if job.t == 0 else (256 if job.kind == "C" else 640) - w
                if job.kind == "C":
                    L = b_["L"][:, n % 3, :].rearrange("p (h x) -> p h x", h=4)[:, :, 0:w]
                    S = s_banks[n % 2][:, :].rearrange("p (h x) -> p h x", h=4)[:, :, 0:w]
                    mk = c_mask[:, first_col:first_col + w].rearrange("p (o x) -> p o x", o=1).to_broadcast([P, 4, w])
                    dve.tensor_tensor(L, S, mk, ALU.add).then_inc(s.logit, 1)
                    dve.wait_ge(s.logit, n + 1)
                    dve.tensor_reduce(raw_max[:, n % 4, :], L, AX.X, ALU.max, negate=True).then_inc(s.mx0, 1)
                    dve.wait_ge(s.mx0, n + 1)
                    sk = neg_sinks[:, 4 * i:4 * i + 4]
                    dve.scalar_tensor_tensor(neg_max[:, n % 4, :], raw_max[:, n % 4, :], HD ** -0.5, sk,
                                             ALU.mult, ALU.min).then_inc(s.mx, 1)
                    dve.wait_ge(s.mx, 2 * n + 1)
                    dve.tensor_tensor(raw_max[:, n % 4, :], neg_max[:, n % 4, :], sk, ALU.subtract).then_inc(s.mx, 1)
                    return
                if job.kind == "B":
                    add = bias[:, i, first_col:first_col + w]
                elif job.t in (1, 2):
                    add = band_mask[:, first_col:first_col + w]
                else:
                    if i == 0:
                        dve.wait_ge(mask_made, 1 + TOPK_TILES.index(job.t))
                    add = score[:, SCORE_OFF[job.t]:SCORE_OFF[job.t] + w]
                dve.tensor_tensor_reduce(b_["L"][:, n % 3, 0:w], s_banks[n % 2][:, 0:w], add, -HD ** -0.5, 3e38,
                                         ALU.add, ALU.min, neg_max[:, n % 4, 0:1]).then_inc(s.logit, 1)

            def out_lo(use):
                _, j, i = use
                job = plan.jobs[j]
                dve.wait_ge(s.o_hi, plan.count("o", use))
                c0, c1 = tile_cols(job.t)
                if job.t == 0:
                    c1 = SAMPLE
                k0 = 4 if job.kind == "B" else 4 * i
                src = bank(7).rearrange("p (a b) -> p a b", a=4)[:, :, 0:c1 - c0]
                dve.tensor_tensor(act_lo[:, k0:k0 + 4, c0:c1], src, act_hi[:, k0:k0 + 4, c0:c1].bitcast(F32),
                                  ALU.subtract).then_inc(s.o_lo, 1)

            if layer == 0:
                dve.wait_ge(bias_in, 16)
                for h in range(8):
                    ins = dve.scalar_tensor_tensor(bias[:, h, :], bias[:, h, :], HD ** 0.5, band_mask[:], ALU.mult, ALU.add)
                ins.then_inc(bias_made, 1)
                dve.wait_ge(bias_made, 1)
            for i in range(3):
                ins = dve.memset(b_["L"][:, i, :], 0.0)
            ins.then_inc(L_clear, 1)
            dve.wait_ge(L_clear, layer + 1)
            for n in range(n_steps + 4):
                if 0 <= n - 3 < n_steps:
                    scale_out(n - 3)
                if n < n_steps:
                    mask_logits(n)
                if layer == 0:
                    for r in range(rounds_by_step(n - 1, done), rounds_by_step(n, done)):
                        topk_round(dve, r)
                for use in plan.at_slot(n):
                    if use[0] == "o":
                        out_lo(use)

        L_clear = sem("L_clear")
        asem[1].mx0 = sem("raw_mx")

        def dve_out_project(dve, layer):
            for hf in range(2):
                for nn in range(4):
                    n = 4 * hf + nn
                    if layer == 0:
                        dve.wait_ge(xt_in[n // 2], 64)
                    for c, (c0, w) in enumerate(CUTS):
                        v = 3 * n + c
                        dve.wait_ge(out_mm, 24 * layer + v + 1)
                        x = xT[:, n, c0:c0 + w]
                        dve.tensor_tensor(x, x, bank(v % 4)[:, 0:w], ALU.add).then_inc(out_add, 1)

        def dve_ffn(dve, layer):
            ub, db = 6 * FGROUPS * layer, 24 * FGROUPS * layer

            def pieces(par, n):
                for q in range(6):
                    f, c = divmod(q, 3)
                    c0, w = CUTS[c]
                    s_ = silu_out[:, q % 2, 0:w]
                    dve.wait_ge(silu_made, n + (q + 1))
                    dve.tensor_tensor(s_, s_, bank(2 * (q % 2) + 1)[:, 0:w], ALU.mult).then_inc(h_made, 1)
                    dve.wait_ge(h_hi_made, n + (q + 1))
                    dve.tensor_tensor(h_lo(par, f)[:, c0:c0 + w], s_, h_hi(par, f)[:, c0:c0 + w].bitcast(F32),
                                      ALU.subtract).then_inc(h_lo_made, 1)

            def adds(d, last):
                for m in range(KT):
                    for c, (c0, w) in enumerate(CUTS):
                        v = 3 * m + c
                        dve.wait_ge(dn_mm, d + (v + 1))
                        x = xT[:, m, c0:c0 + w]
                        ps = bank(v % 4) if last else bank(4 + v % 4)
                        dve.tensor_tensor(x, x, ps[:, 0:w], ALU.add).then_inc(dn_add, 1)

            pieces(0, ub)
            with dve.Fori(0, (FGROUPS - 1) // 2) as it:
                for half in range(2):
                    pieces((half + 1) % 2, it * 12 + (ub + 6 * (half + 1)))
                    adds(it * 48 + (db + 24 * half), False)
            adds(db + 24 * (FGROUPS - 1), True)

        @block.vector
        def _(dve):
            dve.memset(ones[:], 1.0).then_inc(dve_init, 1)
            dve.wait_ge(const_in, 16 * len(CONSTS))
            dve.tensor_scalar(neg_sinks[:], sinks[:], -1.0, None, ALU.mult)
            dve_norm_rest(dve, 0)
            dve_project(dve, 0)
            wait_group(dve, OUT0 - 1)
            dve.wait_ge(piece_add, len(PIECES))
            for i in range(3):
                wait_stored(dve, 0, len(UNITS[0]) - 1 - i)
            dve_attention(dve, 0)
            dve_out_project(dve, 0)
            dve_norm_rest(dve, 1)
            dve_ffn(dve, 0)
            dve_norm_rest(dve, 2)
            dve_project(dve, 1)
            wait_group(dve, OUT1 - 1)
            for i in range(3):
                wait_stored(dve, 1, len(UNITS[1]) - 1 - i)
            dve_attention(dve, 1)
            dve_out_project(dve, 1)
            dve_norm_rest(dve, 3)
            dve_ffn(dve, 1)


def _layout(i):
    f = np.float32
    d = {}
    x = np.concatenate([np.asarray(i["x_sample"])[0], np.asarray(i["x_prompt"])[0]], 0)
    d["xT"] = np.ascontiguousarray(x.T).reshape(KT, P, NTOK)
    w = np.asarray(i["w_in_even"])[0]

    def cols(a0, heads):
        return np.concatenate([np.arange(a0 + HD * h, a0 + HD * h + HD) for h in heads])

    pair_a, pair_c = [0, 4, 1, 5, 2, 6, 3, 7], [x for h in range(8) for x in (h, h + 8)]
    order = np.concatenate([np.arange(1280, 1344), np.arange(512, 768), np.arange(1344, 1352),
                            np.arange(768, 1280), cols(0, pair_a), np.arange(1352, 2888)])

    def by_rows(m):
        return np.ascontiguousarray(m.reshape(-1, P, m.shape[1]).transpose(1, 0, 2))

    d["w_even"] = by_rows(w[:, order])
    wo = np.asarray(i["w_in_odd"])[0]
    d["w_odd"] = by_rows(wo[:, np.concatenate([cols(0, pair_c), np.arange(1024, 1280)])])
    d["w_out0"] = by_rows(np.asarray(i["w_out_even"])[0])
    d["w_out1"] = by_rows(np.asarray(i["w_out_odd"])[0])
    w1, w2 = np.asarray(i["w_ffn_in"]), np.asarray(i["w_ffn_out"])
    w1 = w1.reshape(2, KT, P, 2, FGROUPS, 256).transpose(0, 4, 2, 1, 3, 5)
    d["w_up"] = np.ascontiguousarray(w1).reshape(2, FGROUPS, P, KT, 512)
    w2 = w2.reshape(2, FGROUPS, 2, P, 2, 512).transpose(0, 1, 3, 2, 4, 5)
    d["w_down"] = np.ascontiguousarray(w2).reshape(2, FGROUPS, P, 4, 512)

    pos = np.zeros((TILES, P), f)
    pos[0] = np.concatenate([PAST + np.arange(SAMPLE), np.arange(P - SAMPLE)])
    for t in range(1, TILES):
        pos[t] = P * (t - 1) + np.arange(P)
    inv = (f(10000.0) ** (-np.arange(32, dtype=f) / f(32))).astype(f)
    ang = (pos[:, :, None] * inv[None, None, :]).astype(f)
    c, s = np.cos(ang).astype(f), np.sin(ang).astype(f)
    d["cos"] = np.ascontiguousarray(np.concatenate([c, c], -1).transpose(1, 0, 2))
    d["sin"] = np.ascontiguousarray(np.concatenate([-s, s], -1).transpose(1, 0, 2))
    row, col = np.arange(P)[:, None] // CHUNK, np.arange(640)[None, :] // CHUNK
    d["band_mask"] = np.where((col >= row) & (col <= 8 + row), 0.0, MASKED).astype(f)
    col = np.arange(256)[None, :] // CHUNK
    d["c_mask"] = np.where((col >= row) & (col <= 2 + row), 0.0, MASKED).astype(f)
    d["ident"] = np.eye(P, dtype=f)

    def rows(v):
        return np.ascontiguousarray(np.broadcast_to(np.asarray(v), (P, len(v))))

    def swap(v):
        return np.concatenate([np.roll(v[k:k + HD], 32) for k in range(0, len(v), HD)])

    g = {n: np.asarray(i[k])[0] for n, k in (("aq", "a_q_norm"), ("ak", "a_k_norm"), ("ik", "idx_k_norm"),
         ("bq", "b_q_norm"), ("bk", "b_k_norm"), ("cq", "c_q_norm"), ("ck", "c_k_norm"))}
    g["ikv"] = np.concatenate([g.pop("ik"), g["ak"], g.pop("ak")])
    for n, v in g.items():
        d[f"gain_{n}"] = rows(v)
        if n not in ("bq", "bk"):
            d[f"gainsw_{n}"] = rows(swap(v))
    nm, nf = np.asarray(i["norm_mix"]), np.asarray(i["norm_ffn"])
    ng = np.stack([nm[0], nf[0], nm[1], nf[1]]).reshape(4, KT, P)
    d["norm_gain"] = np.ascontiguousarray(ng.transpose(2, 0, 1))
    d["sinks"] = rows(np.asarray(i["c_sinks"])[0])
    rel = np.clip(np.arange(640)[None, :] - 512 - np.arange(P)[:, None], -128, 128) + 128
    d["bias"] = np.ascontiguousarray(np.asarray(i["b_rel_bias"])[0][:, rel].transpose(1, 0, 2))
    d["cache_a_kidxT"] = np.ascontiguousarray(np.asarray(i["cache_a_kidx"])[0, 0].T)
    d["cache_a_kT"] = np.ascontiguousarray(np.asarray(i["cache_a_k"])[0, 0].reshape(PAST, 128).T)
    blocks = lambda m: np.ascontiguousarray(m.reshape(-1, P, m.shape[-1]).transpose(1, 0, 2))
    d["cache_a_v"] = blocks(np.asarray(i["cache_a_v"])[0, 0].reshape(PAST, 128))
    kb = np.asarray(i["cache_b_k"])[0, 0].reshape(4, P, 4, P)
    d["cache_b_kT"] = np.ascontiguousarray(kb.transpose(3, 2, 0, 1))
    d["cache_b_v"] = blocks(np.asarray(i["cache_b_v"])[0, 0].reshape(PAST, 512))
    d["cache_c_kT"] = np.ascontiguousarray(np.asarray(i["cache_c_k"])[0, 0].reshape(128, 128).T)
    d["cache_c_v"] = np.ascontiguousarray(np.asarray(i["cache_c_v"])[0, 0].reshape(128, 128))
    return d


_OUTS = {"yT": (KT, P, NTOK), "pa_k": (1024, 128), "pa_v": (1024, 128), "pa_kidx": (1024, 64),
         "pb_k": (512, 512), "pb_v": (512, 512), "pc_k": (128, 128), "pc_v": (128, 128),
         "sa_k": (64, 128), "sa_v": (64, 128), "sa_kidx": (64, 64), "sb_k": (64, 512), "sb_v": (64, 512),
         "sc_k": (64, 128), "sc_v": (64, 128)}


def kernel(**inputs):
    import concourse.bacc as bacc
    from concourse.bass_utils import run_bass_kernel_spmd

    arrays = _layout(inputs)
    nc = bacc.Bacc("TRN2", target_bir_lowering=False, num_devices=1, dynamic_dma_scratch_size=1024)
    a = {n: nc.dram_tensor(f"in_{n}", list(v.shape), F32, kind="ExternalInput").ap() for n, v in arrays.items()}
    a.update({n: nc.dram_tensor(f"out_{n}", list(s), F32, kind="ExternalOutput").ap() for n, s in _OUTS.items()})
    build(nc, a)
    r = run_bass_kernel_spmd(nc, [{f"in_{n}": v for n, v in arrays.items()}], core_ids=[0]).results[0]
    o = {n: r[f"out_{n}"] for n in _OUTS}
    y = o["yT"].reshape(D, NTOK).T
    y_s, y_p = y[:SAMPLE][None], y[SAMPLE:][None]

    def heads(x, h):
        return x.reshape(1, 1, x.shape[0], h, HD)

    def both(p):
        return (heads(o[p + "a_k"], 2), heads(o[p + "a_v"], 2), o[p + "a_kidx"][None, None],
                heads(o[p + "b_k"], 8), heads(o[p + "b_v"], 8), heads(o[p + "c_k"], 2), heads(o[p + "c_v"], 2))

    return (y_p, y_s) + both("p") + both("s")
```

```python
from contextlib import ExitStack

import concourse.bass as bass
import numpy as np
from concourse import mybir

F32 = mybir.dt.float32
F32R = mybir.dt.float32r
ALU = mybir.AluOpType
ACT = mybir.ActivationFunctionType
AX = mybir.AxisListType

P = 128
D = 1024
KT = D // P
CHUNK = 64
HD = 64
SAMPLE, PROMPT, PAST = 64, 1024, 512
NTOK = SAMPLE + PROMPT
TILES = 1 + PROMPT // P
CUTS = [(0, 384), (384, 352), (736, 352)]
EPS = 1e-6
D_FF = 2816
FGROUPS = D_FF // 256
TOPK_P, TOPK_S = 256, 144
MASKED = -1e30
TAKEN = -3e38
SW = 512
IDX_SCALE = 512 ** -0.5

EVEN_GROUPS = [("ikv", 328, 3, 3), ("iq", 512, 0, 8), ("aq", 512, 8, 8),
               ("bq", 512, 8, 0), ("bk", 512, 8, 0), ("bv", 512, 0, 0)]
ODD_GROUPS = [("cq0", 512, 8, 8), ("cq1", 512, 8, 8), ("ckv", 256, 2, 2)]


def tile_cols(t):
    return (0, P) if t == 0 else (SAMPLE + P * (t - 1), SAMPLE + P * t)


def cuts_for(col_end):
    return 1 + max(i for i, (c0, _) in enumerate(CUTS) if c0 < col_end)


TOPK_TILES = [0] + list(range(3, TILES))


def score_width(t):
    return PAST + SAMPLE if t == 0 else P * t


PIECES = []
for _t in TOPK_TILES:
    _n = score_width(_t)
    _parts = [(0, _n)] if _n <= 512 else [(0, _n // 2), (_n // 2, _n // 2)]
    for _h in range(8):
        for _i, (_c, _w) in enumerate(_parts):
            PIECES.append((_t, _h, _c, _w, _h == 7 and _i == len(_parts) - 1))
PIECE_END = {p[0]: i + 1 for i, p in enumerate(PIECES)}
SCORE_OFF = {}
_o = 0
for _t in TOPK_TILES:
    SCORE_OFF[_t] = _o
    _o += score_width(_t)
SCORE_COLS = _o
ROUNDS = []
for _t in TOPK_TILES:
    _r = (TOPK_S if _t == 0 else TOPK_P) // 8
    ROUNDS += [(_t, i == _r - 1) for i in range(_r)]
ROUND_END = {r[0]: i + 1 for i, r in enumerate(ROUNDS)}
FIRST_PIECE_UNIT = 12


def pieces_by(u):
    return min(len(PIECES), max(0, (u - FIRST_PIECE_UNIT + 1) * 7 // 2))


class Job:
    def __init__(self, kind, t):
        self.kind, self.t = kind, t
        self.heads = 16 if kind == "C" else 8
        self.group = 4 if kind == "C" else 1
        self.steps = self.heads // self.group
        if kind == "A":
            self.blocks = list(range(8, 13)) if t == 0 else list(range(t))
        elif kind == "B":
            self.blocks = list(range(8, 13)) if t == 0 else list(range(max(0, t - 5), t))
        else:
            self.blocks = [8, 9] if t == 0 else list(range(max(0, t - 2), t))
        self.width = P * len(self.blocks) - (P - SAMPLE if t == 0 else 0)


EVEN_JOBS = [Job(k, t) for k, t in [("A", 1), ("A", 2), ("B", 0), ("B", 1), ("A", 0), ("B", 2), ("A", 3),
             ("B", 3), ("A", 4), ("B", 4), ("A", 5), ("B", 5), ("B", 6), ("A", 6), ("B", 7), ("A", 7),
             ("B", 8), ("A", 8)]]
ODD_JOBS = [Job("C", t) for t in range(TILES)]


TR_LAG, PV_LAG, OUT_LAG = 2, 3, 4


class Plan:

    def __init__(self, jobs):
        self.jobs = jobs
        self.steps = [(j, i) for j, job in enumerate(jobs) for i in range(job.steps)]
        self.first = [sum(x.steps for x in jobs[:j]) for j in range(len(jobs) + 1)]
        self.pt_groups = []
        for j, i in self.steps:
            job = jobs[j]
            units = [(g, b) for g in range(job.group) for b in range(len(job.blocks))]
            self.pt_groups.append([units[k:k + 4] for k in range(0, len(units), 4)])
        self.pt_base = [sum(len(g) for g in self.pt_groups[:s]) for s in range(len(self.steps) + 1)]
        self.early = {s: [] for s in range(-1, len(self.steps) + OUT_LAG + 1)}
        self.late = {s: [] for s in self.early}
        self.early[-1] = self.bank_uses(0, "q") + self.bank_uses(0, "k")
        for j, job in enumerate(jobs):
            f, e = self.first[j], self.first[j + 1]
            if job.kind == "C":
                if j + 1 < len(jobs):
                    self.early[f] += [("q", j + 1, 0)]
                    self.early[f + 1] += [("q", j + 1, 1)]
                    self.early[f + 2] += [("k", j + 1, 0)]
                self.late[e + 1] += [("o", j, 0)]
                self.early[e + 3] += [("o", j, 1)]
            else:
                if j + 1 < len(jobs):
                    self.early[f + 4] += [("q", j + 1, 0)]
                    self.early[f + 5] += [("k", j + 1, 0)]
                self.early[e + 3] += [("o", j, 0)]
        self.uses = []
        for s in self.early:
            self.uses += self.early[s] + self.late[s]
        self.use_no = {u: n for n, u in enumerate(self.uses)}

    def bank_uses(self, j, what):
        job = self.jobs[j]
        if what == "k":
            return [("k", j, 0)]
        return [(what, j, i) for i in range(2 if job.kind == "C" else 1)]

    def scaled_by(self, use):
        _, j, i = use
        job = self.jobs[j]
        return self.first[j] + (i + 1) * job.steps // (2 if job.kind == "C" else 1)

    def count(self, kinds, use):
        return sum(1 for u in self.uses[:self.use_no[use] + 1] if u[0] in kinds)


EVEN_PLAN, ODD_PLAN = Plan(EVEN_JOBS), Plan(ODD_JOBS)


def round_cost(r):
    return 2 * score_width(ROUNDS[r][0]) + 300


def spread_over_units():
    done, out, credit = 0, [], 0
    for u in range(len(EVEN_GROUPS) * TILES):
        _, width, nh, nr = EVEN_GROUPS[u // TILES]
        made = [PIECES[i][3] for i in range(pieces_by(u - 1), pieces_by(u))]
        pe_time = 10 * width + sum(1.7 * w for w in made)
        cols = HD * max(nh, nr) if nh or nr else width
        passes = 1 + 2 * bool(nh) + 3 * bool(nr)
        credit = min(credit, 3000) + pe_time * UNIT_SHARE - passes * cols - 500
        while done < len(ROUNDS) and credit > 0 and pieces_by(u - 2) >= PIECE_END[ROUNDS[done][0]]:
            credit -= round_cost(done)
            done += 1
        out.append(done)
    return out


def spread_over_steps(done):
    free, start = [], {}
    for s, (j, i) in enumerate(EVEN_PLAN.steps):
        job = EVEN_PLAN.jobs[j]
        if job.kind == "A" and i == 0:
            start[job.t] = s
        free.append(max(530 * len(job.blocks) - 1.1 * job.width - 400, 50))
    last = max(start[t] for t in TOPK_TILES) - 1
    todo = sum(round_cost(r) for r in range(done, len(ROUNDS)))
    ratio, credit, out = todo / sum(free[:last]), 0, []
    for s in range(len(free)):
        credit += free[s] * ratio
        due = max([ROUND_END[t] for t in TOPK_TILES if start[t] <= s + 1] + [0])
        while done < len(ROUNDS) and (credit > 0 or done < due):
            credit -= round_cost(done)
            done += 1
        out.append(done)
    return out


UNIT_SHARE = 0.85
ROUNDS_BY_UNIT = spread_over_units()
ROUNDS_BY_STEP = spread_over_steps(ROUNDS_BY_UNIT[-1])


def band_block(b):
    return (b - 8 if b >= 8 else 5 + b) % 6


def build(nc, a):
    ctx = ExitStack()
    with ctx:
        base = (nc.sbuf_base + 63) // 64 * 64
        top = nc.sbuf_usable_end
        RING = 16

        class Region:

            def __init__(self, *spans):
                self.spans = [list(s) for s in spans]

            def cut(self, name, shape, dt=F32):
                size = (int(np.prod(shape[1:])) * 4 + 31) // 32 * 32
                for s in self.spans:
                    if s[1] - s[0] >= size:
                        t = nc.alloc_sbuf_tensor_at(name, shape, dt, offset=s[0])
                        s[0] += size
                        return t
                raise ValueError(f"no room for {name}: {size} in {self.spans}")

        whole = Region((base, top))
        cos = whole.cut("cos", [P, TILES, HD])
        sin = whole.cut("sin", [P, TILES, HD])
        band_mask = whole.cut("band_mask", [P, 640])
        ident = whole.cut("ident", [P, P])
        ones = whole.cut("ones", [P, P])
        gains = {n: whole.cut(f"gain_{n}", [P, w]) for n, w in
                 (("ikv", 192), ("aq", 64), ("bq", 64), ("bk", 64), ("cq", 64), ("ck", 64))}
        gains_sw = {n: whole.cut(f"gainsw_{n}", [P, w]) for n, w in
                    (("ikv", 192), ("aq", 64), ("cq", 64), ("ck", 64))}
        norm_gain = whole.cut("norm_gain", [P, 4, KT])
        neg_half = whole.cut("neg_half", [P, 8])
        idx_w = whole.cut("idx_w", [P, TILES, 8])
        neg_sinks = whole.cut("neg_sinks", [P, 16])
        head_ss = whole.cut("head_ss", [P, 2, 8])
        head_rstd = whole.cut("head_rstd", [P, 2, 8])
        cos_g = whole.cut("cos_g", [P, 2, 192])
        sin_g = whole.cut("sin_g", [P, 2, 192])
        neg_max = whole.cut("neg_max", [P, 6, 4])
        row_sum = whole.cut("row_sum", [P, 6, 4])
        row_inv = whole.cut("row_inv", [P, 2, 4])
        raw_max = whole.cut("raw_max", [P, 6, 4])
        sink_e = whole.cut("sink_e", [P, 6, 4])
        tok_var = whole.cut("tok_var", [P, TILES])
        tok_rstd = whole.cut("tok_rstd", [P, TILES])
        tok_r2 = whole.cut("tok_r2", [P, TILES])
        tok_idx = whole.cut("tok_idx", [P, TILES])
        top8 = whole.cut("top8", [P, 8])
        act_hi = whole.cut("act_hi", [P, KT, NTOK], F32R)
        act_lo = whole.cut("act_lo", [P, KT, NTOK], F32R)
        raw = whole.cut("raw", [P, 4, SW])
        ring_hi_at = whole.spans[0][0]
        ring_hi = whole.cut("ring_hi", [P, RING, SW], F32R)
        ring_lo_at = whole.spans[0][0]
        ring_lo = whole.cut("ring_lo", [P, RING, SW], F32R)
        rest_at = whole.spans[0][0]
        xt_at = (top - KT * NTOK * 4) // 64 * 64
        xT = nc.alloc_sbuf_tensor_at("xT", [P, KT, NTOK], F32, offset=xt_at)
        slot = SW * 4

        rest = Region((rest_at, xt_at))
        hT_hi, hT_lo = [None, None], [None, None]
        hT_hi[0] = nc.alloc_sbuf_tensor_at("hT_hi0", [P, 2, NTOK], F32R, offset=rest_at)
        hT_lo[0] = nc.alloc_sbuf_tensor_at("hT_lo0", [P, 2, NTOK], F32R, offset=rest_at + 8704)
        rest.spans[0][0] += 2 * 8704
        silu_out = rest.cut("silu_out", [P, 2, 384])
        norm_at = rest.spans[0][0]
        hT_hi[1] = nc.alloc_sbuf_tensor_at("hT_hi1", [P, 2, NTOK], F32R, offset=norm_at)
        hT_lo_1_at = ring_lo_at + 12 * slot
        hT_lo[1] = [nc.alloc_sbuf_tensor_at("hT_lo1a", [P, NTOK], F32R, offset=ring_hi_at + 12 * slot),
                    nc.alloc_sbuf_tensor_at("hT_lo1b", [P, NTOK], F32R, offset=hT_lo_1_at)]
        over = Region((norm_at, xt_at))
        n_sq = over.cut("n_sq", [P, 2, 384])
        n_acc = over.cut("n_acc", [P, 384])
        n_var = over.cut("n_var", [P, 384])
        n_rstd = over.cut("n_rstd", [P, 384])
        n_tmp = over.cut("n_tmp", [P, 384])
        n_y = over.cut("n_y", [P, 2, 384])
        n_acc_all = nc.alloc_sbuf_tensor_at("n_acc_all", [P, NTOK], F32, offset=norm_at + 2 * 384 * 4)
        assert norm_at + 8704 <= xt_at

        def h_hi(par, f):
            return hT_hi[par][:, f, :]

        def h_lo(par, f):
            return hT_lo[0][:, f, :] if par == 0 else hT_lo[1][f][:, :]

        pr = Region((rest_at, xt_at))
        p_sq = pr.cut("p_sq", [P, 512])
        p_yn = pr.cut("p_yn", [P, 2, 512])
        p_rot = pr.cut("p_rot", [P, 512])
        p_out = pr.cut("p_out", [P, 3, 512])
        ikT = pr.cut("ikT", [P, 1600])
        relu_w = pr.cut("relu_w", [P, 2, 512])
        relu_o = pr.cut("relu_o", [P, 2, 512])
        xr = Region((xt_at, top))
        score = xr.cut("score", [P, SCORE_COLS])
        iqT = xr.cut("iqT", [P, len(TOPK_TILES), 4, P])
        hi_4, hi_8, hi_16 = [ring_hi_at + x * slot for x in (4, 8, 16)]
        lo_4, lo_8 = [ring_lo_at + x * slot for x in (4, 8)]
        idx_at = rest_at + 7 * 512 * 4
        early_hi, early_lo = Region((hi_4, hi_8)), Region((lo_4, lo_8))
        behind_idx = Region((idx_at, xt_at))
        behind_ring, behind_all = Region((hi_8, hi_16)), Region((lo_8, idx_at))
        stream = Region((xt_at + SCORE_COLS * 4, top))
        eb = {"q_tok": early_hi.cut("q_tok0", [P, 2, 512]), "k_tok": early_hi.cut("k_tok0", [P, 2, 512])}
        v_a = early_lo.cut("v_a", [P, 13, 128])
        eb["qT"] = behind_idx.cut("qT0", [P, 2, 512])
        kT_a = behind_idx.cut("kT_a", [P, 1600])
        eb["o_tok"] = [behind_idx.cut(f"o_tok0_{i}", [P, 512]) for i in range(2)]
        kT_b = behind_ring.cut("kT_b", [P, 4, 6, P])
        eb["L"] = [r.cut(f"L0_{i}", [P, 1024]) for i, r in enumerate((behind_idx, behind_ring, behind_all))]
        eb["PT"] = behind_all.cut("PT0", [P, 2, 1024])
        v_b = stream.cut("v_b", [P, 6, 512])
        bias = [(behind_all if h < 7 else stream).cut(f"bias{h}", [P, 640]) for h in range(8)]
        free_hi, free_lo = Region((hi_8, hi_16)), Region((lo_8, rest_at))
        cb = {"q_tok": free_hi.cut("q_tok1", [P, 2, 1024]), "k_tok": free_hi.cut("k_tok1", [P, 2, 128])}
        v_c = free_hi.cut("v_c", [P, 10, 128])
        c_mask = free_hi.cut("c_mask", [P, 256])
        cb["qT"] = free_lo.cut("qT1", [P, 2, 1024])
        kT_c = free_lo.cut("kT_c", [P, 10, P])
        cb["PT"] = Region((hi_4, hi_8)).cut("PT1", [P, 2, 1024])
        slots_lo, behind_p = Region((lo_4, lo_8)), Region((idx_at, xt_at))
        cb["o_tok"] = [slots_lo.cut(f"o_tok1_{i}", [P, 1024]) for i in range(2)]
        cb["L"] = [behind_p.cut(f"L1_{i}", [P, 1024]) for i in range(3)]

        banks = [ctx.enter_context(nc.psum_tensor(f"bank{i}", [P, 512], F32)) for i in (4, 5, 6, 7)]
        s_banks = [ctx.enter_context(nc.psum_tensor(f"s_banks{i}", [P, 1024], F32)) for i in range(2)]

        def bank(i):
            return s_banks[i // 2][:, 512 * (i % 2):512 * (i % 2) + 512] if i < 4 else banks[i - 4][:, :]

        def sem(name):
            return ctx.enter_context(nc.semaphore(name))

        scr = {n: nc.dram_tensor(f"scratch_{n}", [TILES, P, w], F32, kind="Internal").ap()
               for n, w in (("aq", 512), ("akv", 256), ("bq", 512), ("bk", 512), ("bv", 512),
                            ("cq", 1024), ("ckv", 256))}

        const_in = sem("const_in")
        gain_in = sem("gain_in")
        x_in = [sem(f"x_in{c}") for c in range(6)]
        xt_in = [sem(f"xt_in{i}") for i in range(4)]
        raw_in = [sem(f"raw_in{i}") for i in range(4)]
        hi_done = sem("hi_done")
        lo_done = sem("lo_done")
        dve_init = sem("dve_init")
        sq_made = sem("sq_made")
        sq_acc = sem("sq_acc")
        sq_summed = sem("sq_summed")
        var_made = sem("var_made")
        root_made = sem("root_made")
        y_made = sem("y_made")
        xn_hi = sem("xn_hi")
        xn_lo = [sem("xn_lo_even"), sem("xn_lo_odd")]
        tok_sum = sem("tok_sum")
        tok_mean = sem("tok_mean")
        tok_made = sem("tok_made")
        unit_mm = sem("unit_mm")
        unit_sq = sem("unit_sq")
        unit_ss = sem("unit_ss")
        unit_rstd = sem("unit_rstd")
        unit_tab = sem("unit_tab")
        unit_read = sem("unit_read")
        unit_rot = sem("unit_rot")
        unit_out = sem("unit_out")
        stored = [sem(f"stored{i}") for i in range(3)]
        ixt_mm = sem("ixt_mm")
        ixt_out = sem("ixt_out")
        piece_mm = sem("piece_mm")
        piece_relu = sem("piece_relu")
        piece_w = sem("piece_w")
        piece_add = sem("piece_add")
        idxcache_in = sem("idxcache_in")
        topk_a = sem("topk_a")
        topk_b = sem("topk_b")
        mask_made = sem("mask_made")
        out_mm = sem("out_mm")
        out_add = sem("out_add")
        upf_mm = sem("upf_mm")
        silu_made = sem("silu_made")
        h_made = sem("h_made")
        h_hi_made = sem("h_hi_made")
        h_lo_made = sem("h_lo_made")
        dn_mm = sem("dn_mm")
        dn_add = sem("dn_add")
        y_out = sem("y_out")
        acache_in, bcache_in, bias_in = sem("acache_in"), sem("bcache_in"), sem("bias_in")
        bias_made = sem("bias_made")
        job_in = [sem("job_in0"), sem("job_in1")]
        ccache_in = sem("ccache_in")
        cjob_in = [sem("cjob_in0"), sem("cjob_in1")]

        class AttnSems:
            def __init__(self, n):
                self.qk_mm = sem(f"qk_mm{n}")
                self.logit = sem(f"logit{n}")
                self.mx = sem(f"mx{n}")
                self.prob = sem(f"prob{n}")
                self.pt_mm = sem(f"pt_mm{n}")
                self.pt_out = sem(f"pt_out{n}")
                self.pv_mm = sem(f"pv_mm{n}")
                self.inv = sem(f"inv{n}")
                self.o_made = sem(f"o_made{n}")
                self.tr_mm = sem(f"tr_mm{n}")
                self.qk_out = sem(f"qk_out{n}")
                self.o_hi = sem(f"o_hi{n}")
                self.o_lo = sem(f"o_lo{n}")

        asem = [AttnSems(0), AttnSems(1)]

        def linear_groups(w, widths):
            out, c = [], 0
            for wd in widths:
                out.append([(w[:, k, c:c + wd], wd) for k in range(KT)])
                c += wd
            return out

        groups = (linear_groups(a["w_even"], [g[1] for g in EVEN_GROUPS]) +
                  linear_groups(a["w_out0"], [512, 512]) +
                  linear_groups(a["w_odd"], [g[1] for g in ODD_GROUPS]) +
                  linear_groups(a["w_out1"], [512, 512]))
        EVEN0, OUT0, ODD0, OUT1 = 0, 6, 8, 11
        half_of = [0, 1, 0, 1, 0, 1, 0, 1, 0, 1, 0, 1, 0]
        half_of[OUT1], half_of[OUT1 + 1] = 0, 1
        FFN_SLICES = FGROUPS * 12
        first_slice = [8 * g + (FFN_SLICES if g >= ODD0 else 0) for g in range(len(groups))]
        ffn_slice = [8 * ODD0, 8 * len(groups) + FFN_SLICES]

        def wait_group(eng, g):
            if g < OUT0:
                eng.wait_ge(unit_mm, TILES * (g + 1))
            elif ODD0 <= g < OUT1:
                eng.wait_ge(unit_mm, TILES * (OUT0 + g - ODD0 + 1))
            else:
                layer = int(g >= OUT1)
                eng.wait_ge(out_mm, 24 * layer + (20 if g in (OUT0, OUT1) else 24))

        def group_free(eng, g):
            before = [x for x in range(g) if half_of[x] == half_of[g]]
            if before:
                wait_group(eng, before[-1])
            if g == ODD0:
                eng.wait_ge(upf_mm, 6 * FGROUPS)
            if g == ODD0 + 1:
                eng.wait_ge(dn_mm, 24 * FGROUPS)

        def wait_xn(eng, n, q):
            eng.wait_ge(xn_lo[q % 2], 12 * n + q // 2 + 1)

        def load_slice(eng, i, src, width):
            if i >= 4:
                eng.wait_ge(lo_done, i - 3)
            eng.dma_start(raw[:, i % 4, 0:width], src).then_inc(raw_in[i % 4], 16)

        def split_hi(eng, i, sl, width):
            eng.wait_ge(raw_in[i % 4], 16 * (i // 4 + 1))
            eng.activation(ring_hi[:, sl, 0:width], raw[:, i % 4, 0:width], ACT.Copy).then_inc(hi_done, 1)

        def split_lo(eng, i, sl, width):
            eng.wait_ge(hi_done, i + 1)
            eng.tensor_tensor(ring_lo[:, sl, 0:width], raw[:, i % 4, 0:width],
                              ring_hi[:, sl, 0:width].bitcast(F32), ALU.subtract).then_inc(lo_done, 1)

        def group_slices(fn, eng, g, ks):
            for k in ks:
                src, width = groups[g][k]
                i = first_slice[g] + k
                if fn is load_slice:
                    load_slice(eng, i, src, width)
                else:
                    if fn is split_hi and k == 0:
                        group_free(eng, g)
                    fn(eng, i, 8 * half_of[g] + k, width)

        def proj_units(groups_of):
            return [(g, t) for g in range(len(groups_of)) for t in range(TILES)]

        UNITS = [proj_units(EVEN_GROUPS), proj_units(ODD_GROUPS)]
        UBASE = [0, len(UNITS[0])]

        def stores(layer, u):
            g, t = UNITS[layer][u]
            name = (EVEN_GROUPS, ODD_GROUPS)[layer][g][0]
            out, rows = [], slice(0, SAMPLE if t == 0 else P)
            r0 = P * (t - 1)
            if name == "ikv":
                out.append((scr["akv"][t], (64, 320), slice(0, P)))
                pre, at = ("s", slice(0, 64)) if t == 0 else ("p", slice(r0, r0 + P))
                out.append((a[pre + "a_kidx"][at, :], (0, 64), rows))
                out.append((a[pre + "a_k"][at, :], (64, 192), rows))
                out.append((a[pre + "a_v"][at, :], (192, 320), rows))
            elif name in ("aq", "bq", "bk", "bv"):
                out.append((scr[name][t], (0, 512), slice(0, P)))
                if name in ("bk", "bv") and (t == 0 or t >= 5):
                    at = slice(0, 64) if t == 0 else slice(r0 - 512, r0 - 512 + P)
                    out.append((a[("s" if t == 0 else "p") + "b_" + name[1]][at, :], (0, 512), rows))
            elif name in ("cq0", "cq1"):
                c = 512 * int(name[2])
                out.append((scr["cq"][t][:, c:c + 512], (0, 512), slice(0, P)))
            elif name == "ckv":
                out.append((scr["ckv"][t], (0, 256), slice(0, P)))
                if t in (0, 8):
                    pre = "s" if t == 0 else "p"
                    out.append((a[pre + "c_k"][:, :], (0, 128), rows))
                    out.append((a[pre + "c_v"][:, :], (128, 256), rows))
            return out

        store_count = {}
        per = [0, 0, 0]
        for _l in range(2):
            for _u in range(len(UNITS[_l])):
                per[_u % 3] += len(stores(_l, _u))
                store_count[(_l, _u)] = per[_u % 3]

        def wait_stored(eng, layer, u):
            if store_count[(layer, u)]:
                eng.wait_ge(stored[u % 3], 16 * store_count[(layer, u)])

        ALL_UNITS = [(l, u) for l in range(2) for u in range(len(UNITS[l]))]

        def spec(layer, u):
            g, t = UNITS[layer][u]
            return (EVEN_GROUPS, ODD_GROUPS)[layer][g] + (t,)

        def count_units(pred, layer, u):
            n = 0
            for l, v in ALL_UNITS:
                n += bool(pred(spec(l, v)))
                if (l, v) == (layer, u):
                    return n

        def normed(s):
            return s[2] > 0

        def rotary(s):
            return s[3] > 0

        def copied(s):
            return s[0] in ("ikv", "ckv")

        def gain_of(name):
            return {"cq0": "cq", "cq1": "cq", "ckv": "ck"}.get(name, name)

        block = ctx.enter_context(nc.Block())

        CONSTS = [(cos[:], a["cos"]), (sin[:], a["sin"]), (band_mask[:], a["band_mask"]),
                  (ident[:], a["ident"]), (neg_sinks[:], a["sinks"])]
        CONSTS += [(gains[n][:], a[f"gain_{n}"]) for n in gains]
        CONSTS += [(gains_sw[n][:], a[f"gainsw_{n}"]) for n in gains_sw]
        plans = [EVEN_PLAN, ODD_PLAN]

        def job_loads(layer, j):
            job = plans[layer].jobs[j]
            t, b = job.t, j % 2
            if job.kind == "A":
                vb, rows = (12, 64) if t == 0 else (t - 1, P)
                return [(eb["q_tok"][:, b, :], scr["aq"][t]), (eb["k_tok"][:, b, 0:128], scr["akv"][t][:, 0:128]),
                        (v_a[0:rows, vb, :], scr["akv"][t][0:rows, 128:256])]
            if job.kind == "B":
                vb, rows = (band_block(12), 64) if t == 0 else (band_block(t - 1), P)
                return [(eb["q_tok"][:, b, :], scr["bq"][t]), (eb["k_tok"][:, b, :], scr["bk"][t]),
                        (v_b[0:rows, vb, :], scr["bv"][t][0:rows, :])]
            vb, rows = (9, 64) if t == 0 else (t - 1, P)
            return [(cb["q_tok"][:, b, :], scr["cq"][t]), (cb["k_tok"][:, b, :], scr["ckv"][t][:, 0:128]),
                    (v_c[0:rows, vb, :], scr["ckv"][t][0:rows, 128:256])]

        def job_of(jobs, kind, t):
            return next(j for j, x in enumerate(jobs) if (x.kind, x.t) == (kind, t))

        def wait_job_stored(eng, layer, j):
            job = plans[layer].jobs[j]
            names = {"A": ("ikv", "aq"), "B": ("bq", "bk", "bv"), "C": ("cq0", "cq1", "ckv")}[job.kind]
            for g, group in enumerate((EVEN_GROUPS, ODD_GROUPS)[layer]):
                if group[0] in names:
                    wait_stored(eng, layer, TILES * g + job.t)

        def wait_job_in(eng, layer, j):
            eng.wait_ge((job_in, cjob_in)[layer][j % 2], 48 * (j // 2 + 1))

        def load_job(eng, layer, j):
            plan, s = plans[layer], asem[layer]
            job = plan.jobs[j]
            wait_job_stored(eng, layer, j)
            if j >= 2:
                eng.wait_ge(s.tr_mm, plan.use_no[("k", j - 2, 0)] + 1)
            if job.kind == "B" and job.t >= 2:
                done = job_of(plan.jobs, "B", job.t - 2)
                eng.wait_ge(s.pv_mm, plan.first[done + 1])
            for dst, src in job_loads(layer, j):
                eng.dma_start(dst, src).then_inc((job_in, cjob_in)[layer][j % 2], 16)

        def load_ffn(eng, layer):
            w1, w2 = a["w_up"][layer], a["w_down"][layer]
            first = ffn_slice[layer]

            def up(g, i):
                for k in range(KT):
                    eng.wait_ge(lo_done, i + (k - 3))
                    eng.dma_start(raw[:, k % 4, :], w1[g][:, k, :]).then_inc(raw_in[k % 4], 16)

            def down(g, i):
                for k in range(4):
                    eng.wait_ge(lo_done, i + (k - 3))
                    eng.dma_start(raw[:, k % 4, :], w2[g][:, k, :]).then_inc(raw_in[k % 4], 16)

            up(0, first)
            with eng.Fori(0, (FGROUPS - 1) // 2) as it:
                for half in range(2):
                    i = it * 24 + (first + 8 + 12 * half)
                    up(it * 2 + (half + 1), i)
                    down(it * 2 + half, i + 8)
            down(FGROUPS - 1, first + 8 + 12 * (FGROUPS - 1))

        @block.sync
        def _(sp):
            def load_x(c):
                c0, w = CUTS[c]
                for k in (0, 4):
                    sp.dma_start(xT[:, k:k + 4, c0:c0 + w],
                                 a["xT"][k:k + 4, :, c0:c0 + w].rearrange("k p n -> p k n")).then_inc(x_in[2 * c + k // 4], 16)

            load_x(0)
            sp.dma_start(norm_gain[:], a["norm_gain"]).then_inc(gain_in, 16)
            group_slices(load_slice, sp, 0, range(4))
            load_x(1)
            group_slices(load_slice, sp, 0, range(4, KT))
            load_x(2)
            for dst, src in CONSTS:
                sp.dma_start(dst, src).then_inc(const_in, 16)
            group_slices(load_slice, sp, 1, range(KT))
            wait_xn(sp, 0, 22)
            wait_xn(sp, 0, 23)
            for r in (0, 64):
                sp.dma_start(ikT[r:r + 64, 1024:1536], a["cache_a_kidxT"]).then_inc(idxcache_in, 16)
            for g in range(2, 6):
                group_slices(load_slice, sp, g, range(KT))
            group_slices(load_slice, sp, OUT0, range(4))
            group_slices(load_slice, sp, OUT0, range(4, KT))
            wait_group(sp, OUT0 - 2)
            load_job(sp, 0, 0)
            load_job(sp, 0, 1)
            sp.dma_start(v_a[:, 8:12, :], a["cache_a_v"]).then_inc(acache_in, 16)
            sp.wait_ge(piece_add, len(PIECES))
            sp.dma_start(kT_a[:, 1024:1536], a["cache_a_kT"]).then_inc(acache_in, 16)
            sp.dma_start(v_b[:, 0:4, :], a["cache_b_v"]).then_inc(bcache_in, 16)
            wait_group(sp, OUT0 - 1)
            sp.dma_start(kT_b[:, :, 0:4, :], a["cache_b_kT"]).then_inc(bcache_in, 16)
            u_last = len(UNITS[0]) - 1
            sp.wait_ge(unit_out, u_last + 1)
            for i in range(3):
                wait_stored(sp, 0, u_last - i)
            for h in range(8):
                sp.dma_start(bias[h][:], a["bias"][:, h, :]).then_inc(bias_in, 16)
            for j in range(2, len(EVEN_JOBS)):
                load_job(sp, 0, j)
            pl, s = EVEN_PLAN, asem[0]

            def load_xt(tiles, kind, t):
                end = pl.first[job_of(EVEN_JOBS, kind, t) + 1]
                sp.wait_ge(s.logit, end)
                sp.wait_ge(s.pv_mm, end)
                for i in tiles:
                    sp.dma_start(xT[:, i, :], a["xT"][i]).then_inc(xt_in[i // 2], 16)

            load_xt((0, 1), "A", 6)
            load_xt((2,), "A", 7)
            load_xt((5, 6, 7), "B", 8)
            load_xt((3, 4), "A", 8)
            group_slices(load_slice, sp, OUT0 + 1, range(KT))
            load_ffn(sp, 0)
            for g in range(ODD0, OUT1):
                group_slices(load_slice, sp, g, range(KT))
            group_slices(load_slice, sp, OUT1, range(4))
            group_slices(load_slice, sp, OUT1, range(4, KT))
            wait_group(sp, OUT1 - 2)
            sp.dma_start(kT_c[:, 8, :], a["cache_c_kT"]).then_inc(ccache_in, 16)
            sp.dma_start(v_c[:, 8, :], a["cache_c_v"]).then_inc(ccache_in, 16)
            sp.dma_start(c_mask[:], a["c_mask"]).then_inc(ccache_in, 16)
            for j in range(len(ODD_JOBS)):
                load_job(sp, 1, j)
            group_slices(load_slice, sp, OUT1 + 1, range(KT))
            load_ffn(sp, 1)
            for n in range(KT):
                sp.wait_ge(dn_add, 24 * (2 * FGROUPS - 1) + 3 * n + 3)
                sp.dma_start(a["yT"][n], xT[:, n, :]).then_inc(y_out, 16)
            sp.wait_ge(y_out, 16 * KT)

        def mm3(pe, out, w_hi, w_lo, x_hi, x_lo, first, last):
            pe.matmul(out, w_hi, x_hi, start=first, stop=False)
            pe.matmul(out, w_hi, x_lo, start=False, stop=False)
            return pe.matmul(out, w_lo, x_hi, start=False, stop=last)

        def pe_norm_sum(pe, n, c):
            w = CUTS[c][1]
            pe.wait_ge(sq_acc, 7 * (3 * n + c + 1))
            pe.matmul(bank(5 + c)[:, 0:w], ones[:], n_acc[:, 0:w], start=True, stop=True).then_inc(sq_summed, 1)

        def pe_token_sums(pe, n, c):
            pe.wait_ge(sq_acc, 7 * (3 * n + c + 1))
            for t in range(3 * c, 3 * c + 3):
                c0, c1 = tile_cols(t)
                mm = pe.matmul(bank(5 + c)[:, t:t + 1], n_acc_all[:, c0:c1], ones[:, 0:1], start=True, stop=True)
            mm.then_inc(tok_sum, 1)

        def pe_index_transpose(pe, u):
            v = u - 2
            if not 0 <= v < 2 * TILES:
                return
            g, t = UNITS[0][v]
            if g == 1 and t not in TOPK_TILES:
                return
            n = ixt_no(v)
            pe.wait_ge(unit_out, v + 1)
            if n:
                pe.wait_ge(ixt_out, n)
            if g == 0:
                mm = pe.transpose(bank(3)[0:P, 0:P], ik_pair(v), ident[:])
            else:
                for i in range(4):
                    mm = pe.transpose(bank(3)[:, P * i:P * i + P], p_out[:, v % 3, P * i:P * i + P], ident[:])
            mm.then_inc(ixt_mm, 1)

        def ixt_no(v):
            return sum(1 for x in range(v) if UNITS[0][x][0] == 0 or UNITS[0][x][1] in TOPK_TILES)

        def ik_pair(v):
            return p_out[:, v % 3, 384:512]

        def pe_piece(pe, i):
            t, h, c, w, _ = PIECES[i]
            if i == 0:
                pe.wait_ge(idxcache_in, 32)
            if h == 0 and c == 0:
                pe.wait_ge(ixt_out, ixt_no(TILES + t) + 1)
            if i >= 2:
                pe.wait_ge(piece_relu, i - 1)
            r = 64 * (h % 2)
            k0 = (1024 if t == 0 else 0) + c
            pe.matmul(bank(4 + i % 2)[:, 0:w], iqT[r:r + 64, TOPK_TILES.index(t), h // 2, :],
                      ikT[r:r + 64, k0:k0 + w], start=True, stop=True).then_inc(piece_mm, 1)

        def pe_project(pe, layer, n_norm, g0):
            for u, (g, t) in enumerate(UNITS[layer]):
                width = (EVEN_GROUPS, ODD_GROUPS)[layer][g][1]
                c0, c1 = tile_cols(t)
                uu = UBASE[layer] + u
                if uu >= 3:
                    pe.wait_ge(unit_read, uu - 2)
                if layer and u < 3:
                    pe.wait_ge(dn_add, 24 * FGROUPS - 3 + u)
                out = bank(uu % 3)[:, 0:width]
                for k in range(KT):
                    if g == 0:
                        wait_xn(pe, n_norm, 8 * (cuts_for(c1) - 1) + k)
                    if t == 0:
                        pe.wait_ge(lo_done, first_slice[g0 + g] + k + 1)
                    sl = 8 * half_of[g0 + g] + k
                    pe.matmul(out, act_hi[:, k, c0:c1], ring_hi[:, sl, 0:width], start=(k == 0), stop=False)
                    pe.matmul(out, act_lo[:, k, c0:c1], ring_hi[:, sl, 0:width], start=False, stop=False)
                    mm = pe.matmul(out, act_hi[:, k, c0:c1], ring_lo[:, sl, 0:width], start=False,
                                   stop=(k == KT - 1))
                mm.then_inc(unit_mm, 1)
                if u in (0, 2, 4):
                    pe_token_sums(pe, n_norm, u // 2)
                if layer == 0:
                    if u == 1:
                        pe.wait_ge(const_in, 16 * len(CONSTS))
                    pe_index_transpose(pe, u)
                    for i in range(pieces_by(u - 1), pieces_by(u)):
                        pe_piece(pe, i)

        def key_ops(layer, job, head, b):
            blk = job.blocks[b]
            last_sample = job.t == 0 and b == len(job.blocks) - 1
            rows = SAMPLE if last_sample else P
            if job.kind == "A":
                r, kv = 64 * (head // 4), head // 4
                return kT_a[r:r + 64, P * blk:P * blk + rows], v_a[0:rows, blk, 64 * kv:64 * kv + 64], rows
            if job.kind == "B":
                r, sl = 64 * (head % 2), band_block(blk)
                return kT_b[r:r + 64, head // 2, sl, 0:rows], v_b[0:rows, sl, 64 * head:64 * head + 64], rows
            r, kv = 64 * (head // 8), head // 8
            return kT_c[r:r + 64, blk, 0:rows], v_c[0:rows, blk, 64 * kv:64 * kv + 64], rows

        def q_pair(job, head):
            if job.kind == "A":
                return head % 4, head // 4
            if job.kind == "B":
                return head // 2, head % 2
            return head % 8, head // 8

        def step_heads(job, i):
            return list(range(job.group * i, job.group * i + job.group))

        def stride_of(job):
            return 256 if job.kind == "C" else 0

        def pe_attention(pe, layer):
            plan, s, b_ = plans[layer], asem[layer], (eb, cb)[layer]
            n_steps = len(plan.steps)

            def transposes(use):
                what, j, i = use
                job, n = plan.jobs[j], plan.use_no[use]
                if n:
                    before = plan.uses[n - 1]
                    if before[0] == "o":
                        pe.wait_ge(s.o_lo, plan.count("o", before))
                    else:
                        pe.wait_ge(s.qk_out, plan.count("qk", before))
                if what == "o":
                    pe.wait_ge(s.o_made, plan.scaled_by(use))
                    src, cols = b_["o_tok"][j % 2][:, :], range(512 * i, 512 * i + 512, P)
                elif what == "q":
                    wait_job_in(pe, layer, j)
                    src, cols = b_["q_tok"][:, j % 2, :], range(512 * i, 512 * i + 512, P)
                else:
                    src, cols = b_["k_tok"][:, j % 2, :], range(0, 512 if job.kind == "B" else 128, P)
                for m, c in enumerate(cols):
                    mm = pe.transpose(bank(7)[:, P * m:P * m + P], src[:, c:c + P], ident[:])
                mm.then_inc(s.tr_mm, 1)

            def logits(n):
                j, i = plan.steps[n]
                job = plan.jobs[j]
                if i == 0:
                    pe.wait_ge(s.qk_out, plan.count("qk", ("k", j, 0)))
                if i == 0 and job.t == 0:
                    pe.wait_ge(*{"A": (acache_in, 32), "B": (bcache_in, 32), "C": (ccache_in, 48)}[job.kind])
                if n >= 2:
                    pe.wait_ge(s.logit, n - 1)
                for x, head in enumerate(step_heads(job, i)):
                    pair, half = q_pair(job, head)
                    q = b_["qT"][64 * half:64 * half + 64, j % 2, P * pair:P * pair + P]
                    for b in range(len(job.blocks)):
                        kT, _, rows = key_ops(layer, job, head, b)
                        c = stride_of(job) * x + P * b
                        mm = pe.matmul(s_banks[n % 2][:, c:c + rows], q, kT, start=True, stop=True)
                mm.then_inc(s.qk_mm, 1)

            def transpose_probs(n):
                j, i = plan.steps[n]
                job = plan.jobs[j]
                pe.wait_ge(s.prob, n + 1)
                for x, group in enumerate(plan.pt_groups[n]):
                    no = plan.pt_base[n] + x
                    if no >= 2:
                        pe.wait_ge(s.pt_out, no - 1)
                    for m, (g, b) in enumerate(group):
                        c = stride_of(job) * g + P * b
                        mm = pe.transpose(bank(4 + no % 2)[:, P * m:P * m + P], b_["L"][n % 3][:, c:c + P], ident[:])
                    mm.then_inc(s.pt_mm, 1)

            def times_values(n):
                j, i = plan.steps[n]
                job = plan.jobs[j]
                pe.wait_ge(s.pt_out, plan.pt_base[n + 1])
                if i == 0:
                    wait_job_in(pe, layer, j)
                if n:
                    pe.wait_ge(s.o_made, n)
                nb = len(job.blocks)
                for x, head in enumerate(step_heads(job, i)):
                    for b in range(nb):
                        _, v, rows = key_ops(layer, job, head, b)
                        c, o = P * (x * nb + b), 64 * x
                        mm = pe.matmul(bank(6)[:, o:o + 64], b_["PT"][0:rows, n % 2, c:c + P], v,
                                       start=(b == 0), stop=(b == nb - 1))
                mm.then_inc(s.pv_mm, 1)

            pe.wait_ge(unit_read, UBASE[layer] + len(UNITS[layer]))
            if layer == 0:
                pe.wait_ge(piece_relu, len(PIECES))
                pe.wait_ge(ixt_out, ixt_no(2 * TILES))
            for use in plan.early[-1]:
                transposes(use)
            for n in range(n_steps + OUT_LAG + 1):
                if n < n_steps:
                    logits(n)
                for use in plan.early[n]:
                    transposes(use)
                if 0 <= n - TR_LAG < n_steps:
                    transpose_probs(n - TR_LAG)
                if 0 <= n - PV_LAG < n_steps:
                    times_values(n - PV_LAG)
                for use in plan.late[n]:
                    transposes(use)

        def pe_out_project(pe, layer, g0, n_norm):
            plan, s = plans[layer], asem[layer]
            pe.wait_ge(s.o_lo, plan.count("o", plan.uses[-1]))
            for v in range(24):
                c, m = divmod(v, KT)
                c0, w = CUTS[c]
                if v >= 4:
                    pe.wait_ge(out_add, 24 * layer + v - 3)
                for k in range(KT):
                    if v in (0, 4):
                        pe.wait_ge(lo_done, first_slice[g0 + m // 4] + k + 1)
                    sl, col = 8 * half_of[g0 + m // 4] + k, P * (m % 4)
                    mm = mm3(pe, bank(v % 4)[:, 0:w], ring_hi[:, sl, col:col + P], ring_lo[:, sl, col:col + P],
                             act_hi[:, k, c0:c0 + w], act_lo[:, k, c0:c0 + w], k == 0, k == KT - 1)
                mm.then_inc(out_mm, 1)
                if c and m == 0:
                    pe_norm_sum(pe, n_norm, c - 1)

        def down_piece(layer, v, last):
            return (v % KT, v // KT) if last and layer == 0 else (v // 3, v % 3)

        def pe_ffn(pe, layer, n_norm):
            first = ffn_slice[layer]
            ub, hb, db = 6 * FGROUPS * layer, 6 * FGROUPS * layer, 24 * FGROUPS * layer

            def up(par, n, i, peeled):
                for f in range(2):
                    for c, (c0, w) in enumerate(CUTS):
                        q = 3 * f + c
                        if peeled and q < 2:
                            pe.wait_ge(out_add, 24 * layer + 22 + 2 * q)
                        else:
                            pe.wait_ge(h_made, n + (q - 1))
                        for part in range(2):
                            out = bank(2 * (q % 2) + part)[:, 0:w]
                            for k in range(KT):
                                if peeled and f == 0 and part == 0:
                                    wait_xn(pe, n_norm, 8 * c + k)
                                if q == 0 and part == 0:
                                    pe.wait_ge(lo_done, i + (k + 1))
                                col = 256 * part + P * f
                                mm = mm3(pe, out, ring_hi[:, k, col:col + P], ring_lo[:, k, col:col + P],
                                         act_hi[:, k, c0:c0 + w], act_lo[:, k, c0:c0 + w], k == 0, k == KT - 1)
                            if peeled and q == 0 and part == 0:
                                pe_norm_sum(pe, n_norm, 2)
                        mm.then_inc(upf_mm, 1)

            def down(par, n, i, d, last):
                pe.wait_ge(h_lo_made, n)
                for v in range(24):
                    m, c = down_piece(layer, v, last)
                    c0, w = CUTS[c]
                    pe.wait_ge(dn_add, d + (v - 3 if v >= 4 else 0))
                    out = bank(v % 4 if last else 4 + v % 4)[:, 0:w]
                    for f in range(2):
                        if m in (0, 4) and c == 0:
                            pe.wait_ge(lo_done, i + (2 * f + m // 4 + 1))
                        sl = 8 + 2 * f + m // 4
                        col = P * (m % 4)
                        mm = mm3(pe, out, ring_hi[:, sl, col:col + P], ring_lo[:, sl, col:col + P],
                                 h_hi(par, f)[:, c0:c0 + w], h_lo(par, f)[:, c0:c0 + w], f == 0, f == 1)
                    mm.then_inc(dn_mm, 1)

            up(0, ub, first, True)
            with pe.Fori(0, (FGROUPS - 1) // 2) as it:
                for half in range(2):
                    i = it * 24 + (first + 8 + 12 * half)
                    n = it * 12 + (ub + 6 * (half + 1))
                    up((half + 1) % 2, n, i, False)
                    down(half, n, i + 8, it * 48 + (db + 24 * half), False)
            down(0, ub + 6 * FGROUPS, first + 8 + 12 * (FGROUPS - 1), db + 24 * (FGROUPS - 1), True)

        @block.tensor
        def _(pe):
            pe.wait_ge(dve_init, 1)
            pe_project(pe, 0, 0, EVEN0)
            pe_attention(pe, 0)
            pe_out_project(pe, 0, OUT0, 1)
            pe_ffn(pe, 0, 1)
            pe_project(pe, 1, 2, ODD0)
            pe_attention(pe, 1)
            pe_out_project(pe, 1, OUT1, 3)
            pe_ffn(pe, 1, 3)

        TOK_MADE = 4

        def act_norm_square(act, n, q):
            c, k = divmod(q, KT)
            c0, w = CUTS[c]
            if q >= 2:
                c_, k_ = divmod(q - 2, KT)
                act.wait_ge(sq_acc, 21 * n + 7 * c_ + max(k_, 1))
            act.activation(n_sq[:, q % 2, 0:w], xT[:, k, c0:c0 + w], ACT.Square).then_inc(sq_made, 1)

        def act_norm_root(act, n, c):
            w = CUTS[c][1]
            act.wait_ge(var_made, 5 * (3 * (n // 2) + c) + 1)
            act.activation(n_tmp[:, 0:w], n_var[:, 0:w], ACT.Sqrt).then_inc(root_made, 1)

        def act_norm_hi(act, n, q):
            c, k = divmod(q, KT)
            c0, w = CUTS[c]
            act.wait_ge(y_made, 24 * (n // 2) + q + 1)
            act.activation(act_hi[:, k, c0:c0 + w], n_y[:, q % 2, 0:w], ACT.Copy).then_inc(xn_hi, 1)

        def act_norm_behind(act, n, wait_piece, between):
            for v in range(24):
                c, m = divmod(v, KT)
                between(v)
                wait_piece(v)
                act_norm_square(act, n, v)
                if c and m == 1:
                    act_norm_root(act, n, c - 1)
                if c and m >= 2:
                    act_norm_hi(act, n, v - KT - 2)
                if c and m == KT - 1:
                    act_norm_hi(act, n, v - KT - 1)
                    act_norm_hi(act, n, v - KT)
            act_norm_root(act, n, 2)
            for q in range(16, 24):
                act_norm_hi(act, n, q)

        def act_gained_hi(act, n, q):
            c, k = divmod(q, KT)
            c0, w = CUTS[c]
            if q % 2 == 0:
                if q >= 4:
                    wait_xn(act, n, q - 4)
                act.activation(n_y[:, q // 2 % 2, 0:w], xT[:, k, c0:c0 + w], ACT.Copy, scale=norm_gain[:, n, k:k + 1])
            act.activation(act_hi[:, k, c0:c0 + w], xT[:, k, c0:c0 + w], ACT.Copy,
                           scale=norm_gain[:, n, k:k + 1]).then_inc(xn_hi, 1)

        def act_store(act, layer, v):
            if 0 <= v < len(UNITS[layer]):
                act.wait_ge(unit_out, UBASE[layer] + v + 1)
                for dst, (c0, c1), rows in stores(layer, v):
                    act.dma_start(dst, p_out[rows, v % 3, c0:c1]).then_inc(stored[v % 3], 16)

        def act_project(act, layer, g0):
            n_groups = len((EVEN_GROUPS, ODD_GROUPS)[layer])
            for u, (g, t) in enumerate(UNITS[layer]):
                name, width, nh, nr, _ = spec(layer, u)
                uu = UBASE[layer] + u
                act_store(act, layer, u - 2)
                if nh:
                    act.wait_ge(unit_mm, uu + 1)
                    n = count_units(normed, layer, u)
                    if n > 1:
                        act.wait_ge(unit_ss, n - 1)
                    sq = act.activation(p_sq[:, 0:64 * nh], bank(uu % 3)[:, 0:64 * nh], ACT.Square)
                    if copied((name,)):
                        if u >= 3:
                            wait_stored(act, layer, u - 3)
                        if name == "ikv" and u >= 3:
                            act.wait_ge(ixt_mm, u - 2)
                        c0 = 64 * nh
                        if g == layer * 2:
                            act.wait_ge(tok_made, TOK_MADE * (3 * layer + t // 3 + 1))
                        sq = act.activation(p_out[:, u % 3, c0:c0 + 128], bank(uu % 3)[:, c0:c0 + 128], ACT.Copy,
                                            scale=tok_rstd[:, t:t + 1])
                        if name == "ikv":
                            sq = act.activation(idx_w[:, t, :], bank(uu % 3)[:, 320:328], ACT.Copy,
                                                scale=tok_idx[:, t:t + 1])
                    sq.then_inc(unit_sq, 1)
                if t < KT and g + 1 < n_groups:
                    group_slices(split_hi, act, g0 + g + 1, [t])
                if layer == 0:
                    v = u - 2
                    if 0 <= v < 2 * TILES and (UNITS[0][v][0] == 0 or UNITS[0][v][1] in TOPK_TILES):
                        act.wait_ge(ixt_mm, ixt_no(v) + 1)
                        gg, tt = UNITS[0][v]
                        if gg == 0:
                            dst = ikT[:, 1536:1600] if tt == 0 else ikT[:, P * (tt - 1):P * tt]
                            src = bank(3)[:, 0:SAMPLE if tt == 0 else P]
                        else:
                            dst, src = iqT[:, TOPK_TILES.index(tt), :, :].rearrange("p a b -> p (a b)"), bank(3)
                        act.activation(dst, src, ACT.Copy).then_inc(ixt_out, 1)
                    for i in range(pieces_by(u - 1), pieces_by(u)):
                        tt, h, c, w, _ = PIECES[i]
                        act.wait_ge(piece_mm, i + 1)
                        if i >= 2:
                            act.wait_ge(piece_w, i - 1)
                        act.activation(relu_o[:, i % 2, 0:w], bank(4 + i % 2)[:, 0:w], ACT.Relu).then_inc(piece_relu, 1)
                        act.wait_ge(piece_relu, i + 1)
                        if i >= 2:
                            act.wait_ge(piece_add, i - 1)
                        o = SCORE_OFF[tt] + c
                        dst = relu_w[:, i % 2, 0:w] if h else score[:, o:o + w]
                        act.activation(dst, relu_o[:, i % 2, 0:w], ACT.Copy,
                                       scale=idx_w[:, tt, h:h + 1]).then_inc(piece_w, 1)
            act_store(act, layer, len(UNITS[layer]) - 2)
            act_store(act, layer, len(UNITS[layer]) - 1)

        def act_attention(act, layer):
            plan, s, b_ = plans[layer], asem[layer], (eb, cb)[layer]
            n_steps = len(plan.steps)

            def bank7(use):
                what, j, i = use
                job, n = plan.jobs[j], plan.use_no[use]
                act.wait_ge(s.tr_mm, n + 1)
                if what == "o":
                    c0, c1 = tile_cols(job.t)
                    if job.t == 0:
                        c1 = SAMPLE
                    k0 = 4 if job.kind == "B" else 4 * i
                    src = bank(7).rearrange("p (a b) -> p a b", a=4)[:, :, 0:c1 - c0]
                    act.activation(act_hi[:, k0:k0 + 4, c0:c1], src, ACT.Copy).then_inc(s.o_hi, 1)
                    return
                if what == "q":
                    if j >= 2:
                        act.wait_ge(s.qk_mm, plan.first[j - 1])
                    act.activation(b_["qT"][:, j % 2, 512 * i:512 * i + 512], bank(7), ACT.Copy).then_inc(s.qk_out, 1)
                    return
                cols = SAMPLE if job.t == 0 else P
                if job.kind == "B":
                    if job.t >= 2:
                        act.wait_ge(s.qk_mm, plan.first[job_of(plan.jobs, "B", job.t - 2) + 1])
                    dst = kT_b[:, :, band_block(12 if job.t == 0 else job.t - 1), 0:cols]
                    src = bank(7).rearrange("p (a b) -> p a b", a=4)[:, :, 0:cols]
                elif job.kind == "A":
                    b = 12 if job.t == 0 else job.t - 1
                    dst, src = kT_a[:, P * b:P * b + cols], bank(7)[:, 0:cols]
                else:
                    dst, src = kT_c[:, 9 if job.t == 0 else job.t - 1, 0:cols], bank(7)[:, 0:cols]
                act.activation(dst, src, ACT.Copy).then_inc(s.qk_out, 1)

            for use in plan.early[-1]:
                bank7(use)
            for n in range(n_steps + OUT_LAG + 1):
                for use in plan.early[n]:
                    bank7(use)
                if 0 <= n - TR_LAG < n_steps:
                    m = n - TR_LAG
                    for x, group in enumerate(plan.pt_groups[m]):
                        no = plan.pt_base[m] + x
                        act.wait_ge(s.pt_mm, no + 1)
                        if x == 0 and m >= 2:
                            act.wait_ge(s.pv_mm, m - 1)
                        w = P * len(group)
                        act.activation(b_["PT"][:, m % 2, 512 * x:512 * x + w], bank(4 + no % 2)[:, 0:w],
                                       ACT.Copy).then_inc(s.pt_out, 1)
                for use in plan.late[n]:
                    bank7(use)
                if n < n_steps:
                    j, i = plan.steps[n]
                    job, w = plan.jobs[j], plan.jobs[j].width
                    if job.kind == "C":
                        act.wait_ge(s.mx, 2 * n + 2)
                        for x in range(4):
                            L = b_["L"][n % 3][:, 256 * x:256 * x + w]
                            act.activation(L, L, ACT.Exp, bias=neg_max[:, n % 6, x:x + 1], scale=HD ** -0.5,
                                           accum_out=row_sum[:, n % 6, x:x + 1])
                        act.activation(sink_e[:, n % 6, :], raw_max[:, n % 6, :], ACT.Exp).then_inc(s.prob, 1)
                    else:
                        act.wait_ge(s.logit, n + 1)
                        L = b_["L"][n % 3][:, 0:w]
                        act.activation(L, L, ACT.Exp, bias=neg_max[:, n % 6, 0:1], scale=-1.0,
                                       accum_out=row_sum[:, n % 6, 0:1]).then_inc(s.prob, 1)

        def act_out_project(act, layer, g0, n_norm):
            pl, s = plans[layer], asem[layer]
            act.wait_ge(s.pv_mm, len(pl.steps))
            group_slices(split_hi, act, g0, range(4, KT))
            group_slices(split_hi, act, g0 + 1, range(KT))

            def up_slices(v):
                if v >= 20:
                    if v == 20:
                        wait_group(act, g0)
                    ffn_hi(act, ffn_slice[layer], 0, 2, 2 * (v - 20))

            act_norm_behind(act, n_norm, lambda v: act.wait_ge(out_add, 24 * layer + v + 1), up_slices)

        def ffn_hi(act, i0, sl, n, k0=0):
            for k in range(k0, k0 + n):
                act.wait_ge(raw_in[k % 4], i0 * 4 + 16 * (k // 4 + 1))
                act.activation(ring_hi[:, sl + k, :], raw[:, k % 4, :], ACT.Copy).then_inc(hi_done, 1)

        def act_ffn(act, layer):
            first = ffn_slice[layer]
            ub, db = 6 * FGROUPS * layer, 24 * FGROUPS * layer

            def pieces(par, n, fresh=False):
                for q in range(6):
                    f, c = divmod(q, 3)
                    c0, w = CUTS[c]
                    act.wait_ge(upf_mm, n + (q + 1))
                    if not fresh or q >= 2:
                        act.wait_ge(h_lo_made, n + (q - 1))
                    act.activation(silu_out[:, q % 2, 0:w], bank(2 * (q % 2))[:, 0:w], ACT.Silu).then_inc(silu_made, 1)
                    act.wait_ge(h_made, n + (q + 1))
                    act.activation(h_hi(par, f)[:, c0:c0 + w], silu_out[:, q % 2, 0:w], ACT.Copy).then_inc(h_hi_made, 1)

            wait_group(act, (OUT0, OUT1)[layer] + 1)
            pieces(0, ub, fresh=(layer == 0))
            with act.Fori(0, (FGROUPS - 1) // 2) as it:
                for half in range(2):
                    i = it * 24 + (first + 8 + 12 * half)
                    act.wait_ge(upf_mm, it * 12 + (ub + 6 * (half + 1)))
                    ffn_hi(act, i, 0, 8)
                    act.wait_ge(dn_mm, it * 48 + (db + 24 * half))
                    ffn_hi(act, i + 8, 8, 4)
                    pieces((half + 1) % 2, it * 12 + (ub + 6 * (half + 1)))
            act.wait_ge(dn_mm, db + 24 * (FGROUPS - 1))
            ffn_hi(act, first + 8 + 12 * (FGROUPS - 1), 8, 4)
            if layer == 0:
                group_slices(split_hi, act, ODD0, range(KT))
                for v in range(24):
                    act.wait_ge(dn_add, 24 * (FGROUPS - 1) + v + 1)
                    act_gained_hi(act, 2, v)
                    act_norm_square(act, 2, v)

        @block.scalar
        def _(act):
            act.wait_ge(gain_in, 16)
            for c in range(3):
                for k in range(KT):
                    if k in (0, 4):
                        act.wait_ge(x_in[2 * c + k // 4], 16)
                    act_gained_hi(act, 0, 8 * c + k)
                    if c == 0:
                        group_slices(split_hi, act, 0, [k])
                for k in range(KT):
                    act_norm_square(act, 0, 8 * c + k)
            act_project(act, 0, EVEN0)
            group_slices(split_hi, act, OUT0, range(4))
            act.wait_ge(piece_add, len(PIECES))
            act_attention(act, 0)
            act_out_project(act, 0, OUT0, 1)
            act_ffn(act, 0)
            act_project(act, 1, ODD0)
            group_slices(split_hi, act, OUT1, range(4))
            act_attention(act, 1)
            act_out_project(act, 1, OUT1, 3)
            act_ffn(act, 1)

        def pool_project(pool, layer, g0):
            n_groups = len((EVEN_GROUPS, ODD_GROUPS)[layer])

            def tables(u):
                name, width, nh, nr, t = spec(layer, u)
                if not nr:
                    return
                n = count_units(rotary, layer, u)
                if n > 2:
                    pool.wait_ge(unit_rot, 2 * (n - 2))
                b = n % 2
                if nh == 0:
                    pool.tensor_copy(cos_g[:, b, 0:HD], cos[:, t, :])
                    pool.tensor_copy(sin_g[:, b, 0:HD], sin[:, t, :]).then_inc(unit_tab, 1)
                    return
                gw = 192 if name == "ikv" else 64
                r = gw // 64
                for dst, src, gn in ((cos_g, cos, gains), (sin_g, sin, gains_sw)):
                    ins = pool.tensor_tensor(
                        dst[:, b, 0:gw].rearrange("p (h d) -> p h d", h=r),
                        src[:, t, :].rearrange("p (o d) -> p o d", o=1).to_broadcast([P, r, HD]),
                        gn[gain_of(name)][:, 0:gw].rearrange("p (h d) -> p h d", h=r), ALU.mult)
                ins.then_inc(unit_tab, 1)

            def token_rstd(c):
                ts, done = slice(3 * c, 3 * c + 3), TOK_MADE * (3 * layer + c)
                pool.wait_ge(tok_mean, 3 * layer + c + 1)
                pool.tensor_tensor(tok_rstd[:, ts], tok_var[:, ts], neg_half[:, 0:3], ALU.pow).then_inc(tok_made, 1)
                pool.wait_ge(tok_made, done + 1)
                pool.tensor_tensor(tok_r2[:, ts], tok_rstd[:, ts], tok_rstd[:, ts], ALU.mult).then_inc(tok_made, 1)
                pool.wait_ge(tok_made, done + 2)
                pool.tensor_scalar(tok_r2[:, ts], tok_r2[:, ts], 1.0 / HD, None, ALU.mult).then_inc(tok_made, 1)
                pool.tensor_scalar(tok_idx[:, ts], tok_rstd[:, ts], IDX_SCALE, None, ALU.mult).then_inc(tok_made, 1)
                pool.wait_ge(tok_made, done + TOK_MADE)

            def rstd(u):
                name, width, nh, nr, t = spec(layer, u)
                if not nh:
                    return
                n = count_units(normed, layer, u)
                pool.wait_ge(unit_ss, n)
                b = n % 2
                if n > 2:
                    pool.wait_ge(unit_read, [UBASE[l] + v for l, v in ALL_UNITS if normed(spec(l, v))][n - 3] + 1)
                hr = head_rstd[:, b, 0:nh]
                pool.tensor_scalar(hr, head_ss[:, b, 0:nh], tok_r2[:, t:t + 1], EPS,
                                   ALU.mult, ALU.add).then_inc(unit_rstd, 1)
                pool.wait_ge(unit_rstd, 3 * n - 2)
                pool.tensor_tensor(hr, hr, neg_half[:, 0:nh], ALU.pow).then_inc(unit_rstd, 1)
                pool.wait_ge(unit_rstd, 3 * n - 1)
                pool.tensor_scalar(hr, hr, tok_rstd[:, t:t + 1], None, ALU.mult).then_inc(unit_rstd, 1)

            tables(0)
            for u, (g, t) in enumerate(UNITS[layer]):
                if g == 0 and t % 3 == 0:
                    token_rstd(t // 3)
                rstd(u)
                if u + 1 < len(UNITS[layer]):
                    tables(u + 1)
                if t < KT and g + 1 < n_groups:
                    group_slices(split_lo, pool, g0 + g + 1, [t])
                if layer == 0:
                    for i in range(pieces_by(u - 1), pieces_by(u)):
                        tt, h, c, w, _ = PIECES[i]
                        pool.wait_ge(piece_w, i + 1)
                        if i:
                            pool.wait_ge(piece_add, i)
                        o = SCORE_OFF[tt] + c
                        if h:
                            pool.tensor_tensor(score[:, o:o + w], score[:, o:o + w], relu_w[:, i % 2, 0:w],
                                               ALU.add).then_inc(piece_add, 1)
                        else:
                            if tt and c + w == score_width(tt):
                                sc = score[:, o + w - P:o + w]
                                ins = pool.tensor_tensor(sc, sc, band_mask[:, 512:640], ALU.add)
                            else:
                                ins = pool.engine_nop()
                            ins.then_inc(piece_add, 1)

        def norm_lo(eng, n, q):
            c, k = divmod(q, KT)
            c0, w = CUTS[c]
            eng.wait_ge(xn_hi, 24 * n + q + 1)
            eng.tensor_tensor(act_lo[:, k, c0:c0 + w], n_y[:, q % 2, 0:w],
                              act_hi[:, k, c0:c0 + w].bitcast(F32), ALU.subtract).then_inc(xn_lo[q % 2], 1)

        def gained_lo(eng, n, q):
            c, k = divmod(q, KT)
            c0, w = CUTS[c]
            eng.wait_ge(xn_hi, 24 * n + q + 1)
            if q % 2 == 0:
                eng.tensor_tensor(act_lo[:, k, c0:c0 + w], n_y[:, q // 2 % 2, 0:w],
                                  act_hi[:, k, c0:c0 + w].bitcast(F32), ALU.subtract).then_inc(xn_lo[0], 1)
                return
            eng.scalar_tensor_tensor(act_lo[:, k, c0:c0 + w], xT[:, k, c0:c0 + w], norm_gain[:, n, k:k + 1],
                                     act_hi[:, k, c0:c0 + w].bitcast(F32), ALU.mult,
                                     ALU.subtract).then_inc(xn_lo[q % 2], 1)

        def ffn_lo(pool, i0, sl, n, k0=0):
            for k in range(k0, k0 + n):
                pool.wait_ge(hi_done, i0 + (k + 1))
                pool.tensor_tensor(ring_lo[:, sl + k, :], raw[:, k % 4, :],
                                   ring_hi[:, sl + k, :].bitcast(F32), ALU.subtract).then_inc(lo_done, 1)

        def pool_out_project(pool, layer, g0, n_norm):
            group_slices(split_lo, pool, g0, range(4, KT))
            group_slices(split_lo, pool, g0 + 1, range(KT))
            for q in range(24):
                if 10 <= q < 14:
                    ffn_lo(pool, ffn_slice[layer], 0, 2, 2 * (q - 10))
                if q % 2 == 0:
                    norm_lo(pool, n_norm, q)

        def pool_ffn(pool, layer):
            first = ffn_slice[layer]

            with pool.Fori(0, (FGROUPS - 1) // 2) as it:
                for half in range(2):
                    i = it * 24 + (first + 8 + 12 * half)
                    ffn_lo(pool, i, 0, 8)
                    ffn_lo(pool, i + 8, 8, 4)
            ffn_lo(pool, first + 8 + 12 * (FGROUPS - 1), 8, 4)

        @block.gpsimd
        def _(pool):
            pool.memset(neg_half[:], -0.5)
            for q in range(24):
                if q % 2 == 0:
                    gained_lo(pool, 0, q)
                if q < 8:
                    group_slices(split_lo, pool, 0, [q])
            pool.wait_ge(const_in, 16 * len(CONSTS))
            pool_project(pool, 0, EVEN0)
            group_slices(split_lo, pool, OUT0, range(4))
            pool_out_project(pool, 0, OUT0, 1)
            pool_ffn(pool, 0)
            group_slices(split_lo, pool, ODD0, range(KT))
            for q in range(0, 24, 2):
                gained_lo(pool, 2, q)
            pool_project(pool, 1, ODD0)
            group_slices(split_lo, pool, OUT1, range(4))
            pool_out_project(pool, 1, OUT1, 3)
            pool_ffn(pool, 1)

        def dve_norm_acc(dve, n, c, k):
            if k == 0:
                return
            c0, w = CUTS[c]
            done = 7 * (3 * n + c) + k - 1
            acc = n_acc[:, 0:w] if n % 2 else n_acc_all[:, c0:c0 + w]
            q = 8 * c + k
            dve.wait_ge(sq_made, 24 * n + q + 1)
            if k == 1:
                if n % 2 and c:
                    dve.wait_ge(sq_summed, 3 * (n // 2) + c)
                first = n_sq[:, (q - 1) % 2, 0:w]
            else:
                dve.wait_ge(sq_acc, done)
                first = acc
            dve.tensor_tensor(acc, first, n_sq[:, q % 2, 0:w], ALU.add).then_inc(sq_acc, 1)

        def dve_norm_rstd(dve, n, c):
            w, no = CUTS[c][1], 3 * (n // 2) + c
            done = 5 * no
            var, root, r = n_var[:, 0:w], n_tmp[:, 0:w], n_rstd[:, 0:w]
            dve.wait_ge(sq_summed, no + 1)
            dve.tensor_scalar(var, bank(5 + c)[:, 0:w], 1.0 / D, EPS, ALU.mult, ALU.add).then_inc(var_made, 1)
            dve.wait_ge(root_made, no + 1)
            dve.reciprocal(r, root).then_inc(var_made, 1)
            dve.wait_ge(var_made, done + 2)
            dve.tensor_tensor(var, var, r, ALU.mult).then_inc(var_made, 1)
            dve.wait_ge(var_made, done + 3)
            dve.scalar_tensor_tensor(var, var, -0.5, r, ALU.mult, ALU.mult).then_inc(var_made, 1)
            dve.wait_ge(var_made, done + 4)
            dve.scalar_tensor_tensor(r, var, 1.5, r, ALU.add, ALU.mult).then_inc(var_made, 1)
            dve.wait_ge(var_made, done + 5)

        def dve_norm_y(dve, n, q):
            c, k = divmod(q, KT)
            c0, w = CUTS[c]
            if q >= 2:
                wait_xn(dve, n, q - 2)
            dve.scalar_tensor_tensor(n_y[:, q % 2, 0:w], xT[:, k, c0:c0 + w], norm_gain[:, n, k:k + 1],
                                     n_rstd[:, 0:w], ALU.mult, ALU.mult).then_inc(y_made, 1)

        def dve_norm_behind(dve, n, add):
            def y(q):
                dve_norm_y(dve, n, q)
                if q % 2 == 0 and q:
                    norm_lo(dve, n, q - 1)

            for v in range(24):
                c, m = divmod(v, KT)
                add(v)
                if v:
                    dve_norm_acc(dve, n, *divmod(v - 1, KT))
                if c and m == 1:
                    dve_norm_rstd(dve, n, c - 1)
                if c and m >= 2:
                    y(v - KT - 2)
                if c and m == KT - 1:
                    y(v - KT - 1)
                    y(v - KT)
            dve_norm_acc(dve, n, 2, KT - 1)
            dve_norm_rstd(dve, n, 2)
            for q in range(16, 24):
                y(q)
            norm_lo(dve, n, 23)

        def dve_token_mean(dve, layer, c):
            ts = slice(3 * c, 3 * c + 3)
            dve.wait_ge(tok_sum, 3 * layer + c + 1)
            dve.tensor_scalar(tok_var[:, ts], bank(5 + c)[:, ts], 1.0 / D, EPS, ALU.mult, ALU.add).then_inc(tok_mean, 1)

        def topk_round(dve, r):
            t, last = ROUNDS[r]
            first = r == 0 or ROUNDS[r - 1][0] != t
            sc = score[:, SCORE_OFF[t]:SCORE_OFF[t] + score_width(t)]
            if first:
                dve.wait_ge(piece_add, PIECE_END[t])
            if r:
                dve.wait_ge(topk_b, r)
            dve.max(top8[:], sc).then_inc(topk_a, 1)
            dve.wait_ge(topk_a, r + 1)
            dve.match_replace(sc, top8[:], sc, TAKEN).then_inc(topk_b, 1)
            if last:
                dve.wait_ge(topk_b, r + 1)
                dve.tensor_scalar(sc, sc, TAKEN / 2, MASKED, ALU.is_gt, ALU.mult).then_inc(mask_made, 1)

        def dve_project(dve, layer):
            n_units = len(UNITS[layer])

            def sums(u):
                name, width, nh, nr, t = spec(layer, u)
                if nh:
                    n = count_units(normed, layer, u)
                    dve.wait_ge(unit_sq, n)
                    dve.tensor_reduce(head_ss[:, n % 2, 0:nh], p_sq[:, 0:64 * nh].rearrange("p (h d) -> p h d", h=nh),
                                      AX.X, ALU.add).then_inc(unit_ss, 1)

            def finish(u):
                name, width, nh, nr, t = spec(layer, u)
                uu, ps = UBASE[layer] + u, bank((UBASE[layer] + u) % 3)
                hn = max(nh, nr)
                cols = 64 * hn if hn else width
                if u >= 3:
                    wait_stored(dve, layer, u - 3)
                    if layer == 0 and u - 3 < 2 * TILES:
                        dve.wait_ge(ixt_mm, ixt_no(u - 2))
                out = p_out[:, u % 3, 0:cols]
                yn = p_yn[:, u % 2, 0:cols]

                def heads(x):
                    return x.rearrange("p (h d) -> p h d", h=hn)

                dve.wait_ge(unit_mm, uu + 1)
                if nh:
                    n = count_units(normed, layer, u)
                    dve.wait_ge(unit_rstd, 3 * n)
                    dve.wait_ge(unit_sq, n)
                    r = head_rstd[:, n % 2, 0:hn].rearrange("p (h o) -> p h o", o=1).to_broadcast([P, hn, HD])
                    dve.tensor_tensor(heads(yn), heads(ps[:, 0:cols]), r, ALU.mult).then_inc(unit_read, 1)
                elif nr:
                    dve.tensor_scalar(yn, ps[:, 0:cols], tok_rstd[:, t:t + 1], None, ALU.mult).then_inc(unit_read, 1)
                else:
                    dve.tensor_scalar(out, ps[:, 0:cols], tok_rstd[:, t:t + 1], None, ALU.mult).then_inc(unit_read, 1)
                    dve.wait_ge(unit_read, uu + 1)
                    dve.engine_nop().then_inc(unit_out, 1)
                    return
                dve.wait_ge(unit_read, uu + 1)
                if not nr:
                    g = gains[gain_of(name)][:, 0:64].rearrange("p (o d) -> p o d", o=1).to_broadcast([P, hn, HD])
                    dve.tensor_tensor(heads(out), heads(yn), g, ALU.mult).then_inc(unit_out, 1)
                    return
                n = count_units(rotary, layer, u)
                dve.wait_ge(unit_tab, n)
                if name == "ikv":
                    c_, s_ = heads(cos_g[:, n % 2, 0:192]), heads(sin_g[:, n % 2, 0:192])
                else:
                    c_, s_ = [x[:, n % 2, 0:HD].rearrange("p (o d) -> p o d", o=1).to_broadcast([P, hn, HD])
                              for x in (cos_g, sin_g)]
                dve.tensor_tensor(heads(out), heads(yn), c_, ALU.mult)
                y2, r2 = heads(yn), heads(p_rot[:, 0:cols])
                dve.tensor_tensor(r2[:, :, 0:32], y2[:, :, 32:64], s_[:, :, 0:32], ALU.mult).then_inc(unit_rot, 1)
                dve.tensor_tensor(r2[:, :, 32:64], y2[:, :, 0:32], s_[:, :, 32:64], ALU.mult).then_inc(unit_rot, 1)
                dve.wait_ge(unit_rot, 2 * n)
                ins = dve.tensor_tensor(out, out, p_rot[:, 0:cols], ALU.add)
                if name == "ikv":
                    ins.then_inc(unit_rot2, 1)
                    dve.wait_ge(unit_rot2, u + 1)
                    dve.tensor_copy(p_out[:, u % 3, 384:448], p_out[:, u % 3, 0:64])
                    ins = dve.tensor_copy(p_out[:, u % 3, 448:512], p_out[:, u % 3, 0:64])
                ins.then_inc(unit_out, 1)

            for u in range(n_units):
                if u < TILES and u % 3 == 0:
                    dve_token_mean(dve, layer, u // 3)
                sums(u)
                if u:
                    finish(u - 1)
                if layer == 0:
                    for r in range(ROUNDS_BY_UNIT[u - 1] if u else 0, ROUNDS_BY_UNIT[u]):
                        topk_round(dve, r)
            finish(n_units - 1)

        unit_rot2 = sem("unit_rot2")

        def dve_attention(dve, layer):
            plan, s, b_ = plans[layer], asem[layer], (eb, cb)[layer]
            n_steps = len(plan.steps)

            def scale_out(m):
                j, i = plan.steps[m]
                job = plan.jobs[j]
                g = job.group
                rs = row_sum[:, m % 6, 0:g]
                dve.wait_ge(s.pv_mm, m + 1)
                dve.wait_ge(s.prob, m + 1)
                if job.kind == "C":
                    dve.tensor_tensor(rs, rs, sink_e[:, m % 6, :], ALU.add).then_inc(s.inv, 1)
                    dve.wait_ge(s.inv, 2 * m + 1)
                dve.reciprocal(row_inv[:, m % 2, 0:g], rs).then_inc(s.inv, 1)
                dve.wait_ge(s.inv, (2 if job.kind == "C" else 1) * (m + 1))
                if i == 0 and j >= 2:
                    dve.wait_ge(s.tr_mm, plan.use_no[plan.bank_uses(j - 2, "o")[-1]] + 1)
                out = b_["o_tok"][j % 2][:, 64 * g * i:64 * g * (i + 1)]
                if g == 1:
                    dve.tensor_scalar(out, bank(6)[:, 0:64], row_inv[:, m % 2, 0:1], None, ALU.mult).then_inc(s.o_made, 1)
                else:
                    r = row_inv[:, m % 2, 0:g].rearrange("p (h o) -> p h o", o=1).to_broadcast([P, g, HD])
                    dve.tensor_tensor(out.rearrange("p (h d) -> p h d", h=g),
                                      bank(6)[:, 0:64 * g].rearrange("p (h d) -> p h d", h=g), r,
                                      ALU.mult).then_inc(s.o_made, 1)

            def mask_logits(n):
                j, i = plan.steps[n]
                job, w = plan.jobs[j], plan.jobs[j].width
                dve.wait_ge(s.qk_mm, n + 1)
                if n >= 3:
                    dve.wait_ge(s.pt_mm, plan.pt_base[n - 2])
                first_col = 0 if job.t == 0 else (256 if job.kind == "C" else 640) - w
                if job.kind == "C":
                    L = b_["L"][n % 3][:, :].rearrange("p (h x) -> p h x", h=4)[:, :, 0:w]
                    S = s_banks[n % 2][:, :].rearrange("p (h x) -> p h x", h=4)[:, :, 0:w]
                    mk = c_mask[:, first_col:first_col + w].rearrange("p (o x) -> p o x", o=1).to_broadcast([P, 4, w])
                    dve.tensor_tensor(L, S, mk, ALU.add).then_inc(s.logit, 1)
                    dve.wait_ge(s.logit, n + 1)
                    dve.tensor_reduce(raw_max[:, n % 6, :], L, AX.X, ALU.max, negate=True).then_inc(s.mx0, 1)
                    dve.wait_ge(s.mx0, n + 1)
                    sk = neg_sinks[:, 4 * i:4 * i + 4]
                    dve.scalar_tensor_tensor(neg_max[:, n % 6, :], raw_max[:, n % 6, :], HD ** -0.5, sk,
                                             ALU.mult, ALU.min).then_inc(s.mx, 1)
                    dve.wait_ge(s.mx, 2 * n + 1)
                    dve.tensor_tensor(raw_max[:, n % 6, :], neg_max[:, n % 6, :], sk, ALU.subtract).then_inc(s.mx, 1)
                    return
                if job.kind == "B":
                    if job.t == 0:
                        if i == 0:
                            dve.wait_ge(bias_in, 16 * 8)
                        dve.scalar_tensor_tensor(bias[i][:, :], bias[i][:, :], HD ** 0.5, band_mask[:], ALU.mult,
                                                 ALU.add).then_inc(bias_made, 1)
                        dve.wait_ge(bias_made, i + 1)
                    add = bias[i][:, first_col:first_col + w]
                elif job.t in (1, 2):
                    add = band_mask[:, first_col:first_col + w]
                else:
                    if i == 0:
                        dve.wait_ge(mask_made, 1 + TOPK_TILES.index(job.t))
                    add = score[:, SCORE_OFF[job.t]:SCORE_OFF[job.t] + w]
                dve.tensor_tensor_reduce(b_["L"][n % 3][:, 0:w], s_banks[n % 2][:, 0:w], add, -HD ** -0.5, 3e38,
                                         ALU.add, ALU.min, neg_max[:, n % 6, 0:1]).then_inc(s.logit, 1)

            def out_lo(use):
                _, j, i = use
                job = plan.jobs[j]
                dve.wait_ge(s.o_hi, plan.count("o", use))
                c0, c1 = tile_cols(job.t)
                if job.t == 0:
                    c1 = SAMPLE
                k0 = 4 if job.kind == "B" else 4 * i
                src = bank(7).rearrange("p (a b) -> p a b", a=4)[:, :, 0:c1 - c0]
                dve.tensor_tensor(act_lo[:, k0:k0 + 4, c0:c1], src, act_hi[:, k0:k0 + 4, c0:c1].bitcast(F32),
                                  ALU.subtract).then_inc(s.o_lo, 1)

            for i in range(3):
                if layer == 0:
                    ins = dve.memset(b_["L"][i][:, 512 + SAMPLE:640], 0.0)
                else:
                    ins = dve.memset(b_["L"][i][:, :].rearrange("p (h x) -> p h x", h=4)[:, :, P + SAMPLE:256], 0.0)
            ins.then_inc(L_clear, 1)
            dve.wait_ge(L_clear, layer + 1)
            if layer:
                dve.wait_ge(ccache_in, 48)
            for n in range(n_steps + OUT_LAG + 1):
                if 0 <= n - OUT_LAG < n_steps:
                    scale_out(n - OUT_LAG)
                if n < n_steps:
                    mask_logits(n)
                if layer == 0 and n < n_steps:
                    for r in range(ROUNDS_BY_STEP[n - 1] if n else ROUNDS_BY_UNIT[-1], ROUNDS_BY_STEP[n]):
                        topk_round(dve, r)
                for use in plan.early[n] + plan.late[n]:
                    if use[0] == "o":
                        out_lo(use)

        L_clear = sem("L_clear")
        asem[1].mx0 = sem("raw_mx")

        def dve_out_project(dve, layer, n_norm):
            def add(v):
                c, m = divmod(v, KT)
                c0, w = CUTS[c]
                if layer == 0 and c == 0:
                    dve.wait_ge(xt_in[m // 2], 32)
                dve.wait_ge(out_mm, 24 * layer + v + 1)
                x = xT[:, m, c0:c0 + w]
                dve.tensor_tensor(x, x, bank(v % 4)[:, 0:w], ALU.add).then_inc(out_add, 1)

            dve_norm_behind(dve, n_norm, add)

        def dve_ffn(dve, layer):
            ub, db = 6 * FGROUPS * layer, 24 * FGROUPS * layer

            def pieces(par, n):
                for q in range(6):
                    f, c = divmod(q, 3)
                    c0, w = CUTS[c]
                    s_ = silu_out[:, q % 2, 0:w]
                    dve.wait_ge(silu_made, n + (q + 1))
                    dve.tensor_tensor(s_, s_, bank(2 * (q % 2) + 1)[:, 0:w], ALU.mult).then_inc(h_made, 1)
                    dve.wait_ge(h_hi_made, n + (q + 1))
                    dve.tensor_tensor(h_lo(par, f)[:, c0:c0 + w], s_, h_hi(par, f)[:, c0:c0 + w].bitcast(F32),
                                      ALU.subtract).then_inc(h_lo_made, 1)

            def add(v, d, last):
                m, c = down_piece(layer, v, last)
                c0, w = CUTS[c]
                dve.wait_ge(dn_mm, d + (v + 1))
                x = xT[:, m, c0:c0 + w]
                ps = bank(v % 4) if last else bank(4 + v % 4)
                dve.tensor_tensor(x, x, ps[:, 0:w], ALU.add).then_inc(dn_add, 1)

            pieces(0, ub)
            with dve.Fori(0, (FGROUPS - 1) // 2) as it:
                for half in range(2):
                    pieces((half + 1) % 2, it * 12 + (ub + 6 * (half + 1)))
                    for v in range(24):
                        add(v, it * 48 + (db + 24 * half), False)
            if layer == 0:
                for v in range(24):
                    add(v, db + 24 * (FGROUPS - 1), True)
                    if v:
                        dve_norm_acc(dve, 2, *divmod(v - 1, KT))
                    if v % 2 == 0 and v:
                        gained_lo(dve, 2, v - 1)
                dve_norm_acc(dve, 2, 2, KT - 1)
                gained_lo(dve, 2, 23)
            else:
                for v in range(24):
                    add(v, db + 24 * (FGROUPS - 1), True)

        @block.vector
        def _(dve):
            dve.memset(ones[:], 1.0).then_inc(dve_init, 1)
            dve.wait_ge(gain_in, 16)
            for c in range(3):
                for k in range(1, KT, 2):
                    gained_lo(dve, 0, 8 * c + k)
                for k in range(KT):
                    dve_norm_acc(dve, 0, c, k)
            dve.wait_ge(const_in, 16 * len(CONSTS))
            dve.tensor_scalar(neg_sinks[:], neg_sinks[:], -1.0, None, ALU.mult)
            dve_project(dve, 0)
            dve.wait_ge(piece_add, len(PIECES))
            dve_attention(dve, 0)
            dve_out_project(dve, 0, 1)
            dve_ffn(dve, 0)
            dve_project(dve, 1)
            dve_attention(dve, 1)
            dve_out_project(dve, 1, 3)
            dve_ffn(dve, 1)


def _layout(i):
    f = np.float32
    d = {}
    x = np.concatenate([np.asarray(i["x_sample"])[0], np.asarray(i["x_prompt"])[0]], 0)
    d["xT"] = np.ascontiguousarray(x.T).reshape(KT, P, NTOK)
    w = np.asarray(i["w_in_even"])[0]

    def cols(a0, heads):
        return np.concatenate([np.arange(a0 + HD * h, a0 + HD * h + HD) for h in heads])

    pair_a, pair_c = [0, 4, 1, 5, 2, 6, 3, 7], [x for h in range(8) for x in (h, h + 8)]
    order = np.concatenate([np.arange(1280, 1344), np.arange(512, 768), np.arange(1344, 1352),
                            np.arange(768, 1280), cols(0, pair_a), np.arange(1352, 2888)])

    def by_rows(m):
        return np.ascontiguousarray(m.reshape(-1, P, m.shape[1]).transpose(1, 0, 2))

    d["w_even"] = by_rows(w[:, order])
    wo = np.asarray(i["w_in_odd"])[0]
    d["w_odd"] = by_rows(wo[:, np.concatenate([cols(0, pair_c), np.arange(1024, 1280)])])
    d["w_out0"] = by_rows(np.asarray(i["w_out_even"])[0])
    d["w_out1"] = by_rows(np.asarray(i["w_out_odd"])[0])
    w1, w2 = np.asarray(i["w_ffn_in"]), np.asarray(i["w_ffn_out"])
    w1 = w1.reshape(2, KT, P, 2, FGROUPS, 256).transpose(0, 4, 2, 1, 3, 5)
    d["w_up"] = np.ascontiguousarray(w1).reshape(2, FGROUPS, P, KT, 512)
    w2 = w2.reshape(2, FGROUPS, 2, P, 2, 512).transpose(0, 1, 3, 2, 4, 5)
    d["w_down"] = np.ascontiguousarray(w2).reshape(2, FGROUPS, P, 4, 512)

    pos = np.zeros((TILES, P), f)
    pos[0] = np.concatenate([PAST + np.arange(SAMPLE), np.arange(P - SAMPLE)])
    for t in range(1, TILES):
        pos[t] = P * (t - 1) + np.arange(P)
    inv = (10000.0 ** (-np.arange(32, dtype=np.float64) / 32)).astype(f)
    ang = (pos[:, :, None] * inv[None, None, :]).astype(f)
    c, s = np.cos(ang).astype(f), np.sin(ang).astype(f)
    d["cos"] = np.ascontiguousarray(np.concatenate([c, c], -1).transpose(1, 0, 2))
    d["sin"] = np.ascontiguousarray(np.concatenate([-s, s], -1).transpose(1, 0, 2))
    row, col = np.arange(P)[:, None] // CHUNK, np.arange(640)[None, :] // CHUNK
    d["band_mask"] = np.where((col >= row) & (col <= 8 + row), 0.0, MASKED).astype(f)
    col = np.arange(256)[None, :] // CHUNK
    d["c_mask"] = np.where((col >= row) & (col <= 2 + row), 0.0, MASKED).astype(f)
    d["ident"] = np.eye(P, dtype=f)

    def rows(v):
        return np.ascontiguousarray(np.broadcast_to(np.asarray(v), (P, len(v))))

    def swap(v):
        return np.concatenate([np.roll(v[k:k + HD], 32) for k in range(0, len(v), HD)])

    g = {n: np.asarray(i[k])[0] for n, k in (("aq", "a_q_norm"), ("ak", "a_k_norm"), ("ik", "idx_k_norm"),
         ("bq", "b_q_norm"), ("bk", "b_k_norm"), ("cq", "c_q_norm"), ("ck", "c_k_norm"))}
    g["ikv"] = np.concatenate([g.pop("ik"), g["ak"], g.pop("ak")])
    for n, v in g.items():
        d[f"gain_{n}"] = rows(v)
        if n not in ("bq", "bk"):
            d[f"gainsw_{n}"] = rows(swap(v))
    nm, nf = np.asarray(i["norm_mix"]), np.asarray(i["norm_ffn"])
    ng = np.stack([nm[0], nf[0], nm[1], nf[1]]).reshape(4, KT, P)
    d["norm_gain"] = np.ascontiguousarray(ng.transpose(2, 0, 1))
    d["sinks"] = rows(np.asarray(i["c_sinks"])[0])
    rel = np.clip(np.arange(640)[None, :] - 512 - np.arange(P)[:, None], -128, 128) + 128
    d["bias"] = np.ascontiguousarray(np.asarray(i["b_rel_bias"])[0][:, rel].transpose(1, 0, 2))
    d["cache_a_kidxT"] = np.ascontiguousarray(np.asarray(i["cache_a_kidx"])[0, 0].T)
    d["cache_a_kT"] = np.ascontiguousarray(np.asarray(i["cache_a_k"])[0, 0].reshape(PAST, 128).T)
    blocks = lambda m: np.ascontiguousarray(m.reshape(-1, P, m.shape[-1]).transpose(1, 0, 2))
    d["cache_a_v"] = blocks(np.asarray(i["cache_a_v"])[0, 0].reshape(PAST, 128))
    kb = np.asarray(i["cache_b_k"])[0, 0].reshape(4, P, 4, P)
    d["cache_b_kT"] = np.ascontiguousarray(kb.transpose(3, 2, 0, 1))
    d["cache_b_v"] = blocks(np.asarray(i["cache_b_v"])[0, 0].reshape(PAST, 512))
    d["cache_c_kT"] = np.ascontiguousarray(np.asarray(i["cache_c_k"])[0, 0].reshape(128, 128).T)
    d["cache_c_v"] = np.ascontiguousarray(np.asarray(i["cache_c_v"])[0, 0].reshape(128, 128))
    return d


_OUTS = {"yT": (KT, P, NTOK), "pa_k": (1024, 128), "pa_v": (1024, 128), "pa_kidx": (1024, 64),
         "pb_k": (512, 512), "pb_v": (512, 512), "pc_k": (128, 128), "pc_v": (128, 128),
         "sa_k": (64, 128), "sa_v": (64, 128), "sa_kidx": (64, 64), "sb_k": (64, 512), "sb_v": (64, 512),
         "sc_k": (64, 128), "sc_v": (64, 128)}


def kernel(**inputs):
    import concourse.bacc as bacc
    from concourse.bass_utils import run_bass_kernel_spmd

    arrays = _layout(inputs)
    nc = bacc.Bacc("TRN2", target_bir_lowering=False, num_devices=1, dynamic_dma_scratch_size=1024)
    a = {n: nc.dram_tensor(f"in_{n}", list(v.shape), F32, kind="ExternalInput").ap() for n, v in arrays.items()}
    a.update({n: nc.dram_tensor(f"out_{n}", list(s), F32, kind="ExternalOutput").ap() for n, s in _OUTS.items()})
    build(nc, a)
    r = run_bass_kernel_spmd(nc, [{f"in_{n}": v for n, v in arrays.items()}], core_ids=[0]).results[0]
    o = {n: r[f"out_{n}"] for n in _OUTS}
    y = o["yT"].reshape(D, NTOK).T
    y_s, y_p = y[:SAMPLE][None], y[SAMPLE:][None]

    def heads(x, h):
        return x.reshape(1, 1, x.shape[0], h, HD)

    def both(p):
        return (heads(o[p + "a_k"], 2), heads(o[p + "a_v"], 2), o[p + "a_kidx"][None, None],
                heads(o[p + "b_k"], 8), heads(o[p + "b_v"], 8), heads(o[p + "c_k"], 2), heads(o[p + "c_v"], 2))

    return (y_p, y_s) + both("p") + both("s")
```
